# Optimizing a Trainium2 kernel written in Bass

```python
import jax, jax.numpy as jnp
from jax import lax
import numpy as np

D_MODEL = 1024
BATCH = 1
SEQ = 1024
DEPTH = 1
DEC_BATCH = 8
DEC_SEQ = 8
PAST_LEN = 8192
PAGE_SIZE = 128

D_CONV = D_MODEL
CONV_WIDTH = 31
D_MLSTM = D_MODEL
N_HEADS = 4
HEAD_DIM = D_MLSTM // N_HEADS
CHUNK = 128
D_FF = 2816
N_MOD = 9
N_IN = 2 * D_CONV + 4 * D_MLSTM + 2 * D_MODEL + 2 * N_HEADS
EPS = 1e-6

kernel_name = 'hybrid_conv_mlstm_macaron_step'

def _rmsnorm(x, g):
    xf = x.astype(jnp.float32)
    y = xf * lax.rsqrt(jnp.mean(xf * xf, axis=-1, keepdims=True) + EPS)
    return (y * g.astype(jnp.float32)).astype(x.dtype)

def _layernorm(x, g, b):
    xf = x.astype(jnp.float32)
    mu = jnp.mean(xf, axis=-1, keepdims=True)
    var = jnp.mean(jnp.square(xf - mu), axis=-1, keepdims=True)
    y = (xf - mu) * lax.rsqrt(var + EPS)
    return (y * g.astype(jnp.float32) + b.astype(jnp.float32)).astype(x.dtype)

def _headnorm(h, g):
    y = h * lax.rsqrt(jnp.mean(h * h, axis=-1, keepdims=True) + EPS)
    return y * g.astype(jnp.float32)

def _swiglu(x, w_gate, w_up, w_down):
    return (jax.nn.silu(x @ w_gate) * (x @ w_up)) @ w_down

def _split_cols(p):
    sizes = (D_CONV, D_CONV, D_MLSTM, D_MLSTM, D_MLSTM, D_MLSTM, D_MODEL, D_MODEL, N_HEADS, N_HEADS)
    out, start = [], 0
    for s in sizes:
        out.append(p[..., start:start + s])
        start += s
    return out

def _causal_dwconv(u, buf, w, b):
    full = jnp.concatenate([buf.astype(u.dtype), u], axis=1)
    y = lax.conv_general_dilated(full, w[:, None, :].astype(u.dtype), window_strides=(1,), padding='VALID',
                                 dimension_numbers=('NWC', 'WIO', 'NWC'), feature_group_count=u.shape[-1])
    return y + b, full[:, -(CONV_WIDTH - 1):]

def _mlstm_chunkwise(q, k, v, ig, lf, C0, n0, m0, chunk):
    f32 = jnp.float32
    Bn, T, H, DK = q.shape
    nc = T // chunk
    q = q.astype(f32) * (DK ** -0.5)
    k, v, ig, lf = k.astype(f32), v.astype(f32), ig.astype(f32), lf.astype(f32)

    def to_chunks(a):
        return a.reshape((Bn, nc, chunk) + a.shape[2:]).swapaxes(0, 1)

    causal = jnp.tril(jnp.ones((chunk, chunk), dtype=bool))

    def step(carry, xs):
        C, n, m = carry
        qc, kc, vc, ic, fc = xs
        bcum = jnp.cumsum(fc, axis=1).transpose(0, 2, 1)
        ih = ic.transpose(0, 2, 1)
        dmat = bcum[:, :, :, None] - bcum[:, :, None, :] + ih[:, :, None, :]
        dmat = jnp.where(causal, dmat, -jnp.inf)
        inter = bcum + m[:, :, None]
        m_t = jnp.maximum(inter, jnp.max(dmat, axis=-1))
        w_intra = jnp.exp(dmat - m_t[..., None])
        w_inter = jnp.exp(inter - m_t)
        s = jnp.einsum('blhd,bshd->bhls', qc, kc) * w_intra
        num = jnp.einsum('bhls,bshe->blhe', s, vc) + jnp.einsum('bhl,bhed,blhd->blhe', w_inter, C, qc)
        den = jnp.sum(s, axis=-1) + w_inter * jnp.einsum('bhd,blhd->bhl', n, qc)
        den = jnp.maximum(jnp.abs(den), jnp.exp(-m_t))
        h = num / den.transpose(0, 2, 1)[..., None]
        b_last = bcum[:, :, -1]
        dec = b_last[:, :, None] - bcum + ih
        m_new = jnp.maximum(b_last + m, jnp.max(dec, axis=-1))
        a_prev = jnp.exp(b_last + m - m_new)
        ws = jnp.exp(dec - m_new[..., None])
        C_new = a_prev[..., None, None] * C + jnp.einsum('bhs,bshe,bshd->bhed', ws, vc, kc)
        n_new = a_prev[..., None] * n + jnp.einsum('bhs,bshd->bhd', ws, kc)
        return (C_new, n_new, m_new), h

    init = (C0.astype(f32), n0.astype(f32), m0.astype(f32))
    (C, n, m), hs = lax.scan(step, init, (to_chunks(q), to_chunks(k), to_chunks(v), to_chunks(ig), to_chunks(lf)))
    h = hs.swapaxes(0, 1).reshape(Bn, T, H, v.shape[-1])
    return h, C, n, m

def _layer(x, c, conv_buf, C0, n0, m0, chunk, w_ada, b_ada, norm_ffn1, w1_gate, w1_up, w1_down, norm_mix,
           w_in, b_in, w_dw, b_dw, ln_conv_g, ln_conv_b, w_conv_out, mh_norm, w_mlstm_out, w_out,
           norm_ffn2, w2_gate, w2_up, w2_down):
    Bn, T, _ = x.shape
    mod = jax.nn.silu(c) @ w_ada + b_ada
    sh1, sc1, g1, sh2, sc2, g2, sh3, sc3, g3 = [t[:, None, :] for t in jnp.split(mod, N_MOD, axis=-1)]
    h = _rmsnorm(x, norm_ffn1) * (1 + sc1) + sh1
    x = x + 0.5 * g1 * _swiglu(h, w1_gate, w1_up, w1_down)
    u = _rmsnorm(x, norm_mix) * (1 + sc2) + sh2
    p = u @ w_in + b_in
    ca, cg, q, k, v, o, ga, gb, ip, fp = _split_cols(p)
    glu = ca * jax.nn.sigmoid(cg)
    y, conv_new = _causal_dwconv(glu, conv_buf, w_dw, b_dw)
    a_out = jax.nn.silu(_layernorm(y, ln_conv_g, ln_conv_b)) @ w_conv_out
    heads = lambda t: t.reshape(Bn, T, N_HEADS, HEAD_DIM)
    hm, C, n, m = _mlstm_chunkwise(heads(q), heads(k), heads(v), ip, jax.nn.log_sigmoid(fp), C0, n0, m0, chunk)
    hm = _headnorm(hm, mh_norm).reshape(Bn, T, D_MLSTM).astype(x.dtype)
    b_out = (jax.nn.sigmoid(o) * hm) @ w_mlstm_out
    z = jax.nn.sigmoid(ga) * a_out + jax.nn.sigmoid(gb) * b_out
    x = x + g2 * (z @ w_out)
    h = _rmsnorm(x, norm_ffn2) * (1 + sc3) + sh3
    x = x + 0.5 * g3 * _swiglu(h, w2_gate, w2_up, w2_down)
    return x, conv_new, C, n, m

def setup_inputs(seed: int = 0) -> dict:
    key = jax.random.key(seed)
    keys = list(jax.random.split(key, 40))
    cnt = [0]

    def nrm(shape, scale):
        kk = keys[cnt[0]]
        cnt[0] += 1
        return scale * jax.random.normal(kk, shape, jnp.float32)

    L = DEPTH
    d_in = D_MODEL ** -0.5
    inp = {}
    inp['x_prompt'] = nrm((BATCH, SEQ, D_MODEL), 1.0)
    inp['x_sample'] = nrm((DEC_BATCH, DEC_SEQ, D_MODEL), 1.0)
    inp['c_prompt'] = nrm((BATCH, D_MODEL), 1.0)
    inp['c_sample'] = nrm((DEC_BATCH, D_MODEL), 1.0)
    inp['state_conv'] = nrm((L, DEC_BATCH, CONV_WIDTH - 1, D_CONV), 0.5)
    inp['state_C'] = nrm((L, DEC_BATCH, N_HEADS, HEAD_DIM, HEAD_DIM), 0.5)
    inp['state_n'] = nrm((L, DEC_BATCH, N_HEADS, HEAD_DIM), 0.5)
    inp['state_m'] = nrm((L, DEC_BATCH, N_HEADS), 0.5) + 1.0
    inp['w_ada'] = nrm((L, D_MODEL, N_MOD * D_MODEL), 0.5 * d_in)
    inp['b_ada'] = nrm((L, N_MOD * D_MODEL), 0.02)
    inp['norm_ffn1'] = 1.0 + nrm((L, D_MODEL), 0.02)
    inp['w1_gate'] = nrm((L, D_MODEL, D_FF), d_in)
    inp['w1_up'] = nrm((L, D_MODEL, D_FF), d_in)
    inp['w1_down'] = nrm((L, D_FF, D_MODEL), D_FF ** -0.5)
    inp['norm_mix'] = 1.0 + nrm((L, D_MODEL), 0.02)
    inp['w_in'] = nrm((L, D_MODEL, N_IN), d_in)
    inp['b_in'] = nrm((L, N_IN), 0.02).at[:, -N_HEADS:].add(jnp.linspace(3.0, 6.0, N_HEADS))
    inp['w_dw'] = nrm((L, CONV_WIDTH, D_CONV), CONV_WIDTH ** -0.5)
    inp['b_dw'] = nrm((L, D_CONV), 0.02)
    inp['ln_conv_g'] = 1.0 + nrm((L, D_CONV), 0.02)
    inp['ln_conv_b'] = nrm((L, D_CONV), 0.02)
    inp['w_conv_out'] = nrm((L, D_CONV, D_MODEL), D_CONV ** -0.5)
    inp['mh_norm'] = 1.0 + nrm((L, N_HEADS, HEAD_DIM), 0.02)
    inp['w_mlstm_out'] = nrm((L, D_MLSTM, D_MODEL), D_MLSTM ** -0.5)
    inp['w_out'] = nrm((L, D_MODEL, D_MODEL), d_in)
    inp['norm_ffn2'] = 1.0 + nrm((L, D_MODEL), 0.02)
    inp['w2_gate'] = nrm((L, D_MODEL, D_FF), d_in)
    inp['w2_up'] = nrm((L, D_MODEL, D_FF), d_in)
    inp['w2_down'] = nrm((L, D_FF, D_MODEL), D_FF ** -0.5)
    inp['final_norm'] = 1.0 + nrm((D_MODEL,), 0.02)
    return inp

def reference(x_prompt, x_sample, c_prompt, c_sample, state_conv, state_C, state_n, state_m,
              w_ada, b_ada, norm_ffn1, w1_gate, w1_up, w1_down, norm_mix, w_in, b_in, w_dw, b_dw,
              ln_conv_g, ln_conv_b, w_conv_out, mh_norm, w_mlstm_out, w_out, norm_ffn2, w2_gate, w2_up,
              w2_down, final_norm):
    f32 = jnp.float32
    bp, T = x_prompt.shape[0], x_prompt.shape[1]
    ts = x_sample.shape[1]
    yp, ys = x_prompt, x_sample
    conv_p, C_p, n_p, m_p = [], [], [], []
    conv_s, C_s, n_s, m_s = [], [], [], []
    for l in range(DEPTH):
        wl = (w_ada[l], b_ada[l], norm_ffn1[l], w1_gate[l], w1_up[l], w1_down[l], norm_mix[l], w_in[l], b_in[l],
              w_dw[l], b_dw[l], ln_conv_g[l], ln_conv_b[l], w_conv_out[l], mh_norm[l], w_mlstm_out[l], w_out[l],
              norm_ffn2[l], w2_gate[l], w2_up[l], w2_down[l])
        yp, cv, C, n, m = _layer(yp, c_prompt,
                                 jnp.zeros((bp, CONV_WIDTH - 1, D_CONV), x_prompt.dtype),
                                 jnp.zeros((bp, N_HEADS, HEAD_DIM, HEAD_DIM), f32),
                                 jnp.zeros((bp, N_HEADS, HEAD_DIM), f32),
                                 jnp.zeros((bp, N_HEADS), f32),
                                 min(CHUNK, T), *wl)
        conv_p.append(cv.astype(state_conv.dtype))
        C_p.append(C.astype(state_C.dtype))
        n_p.append(n.astype(state_n.dtype))
        m_p.append(m.astype(state_m.dtype))
        ys, cv, C, n, m = _layer(ys, c_sample, state_conv[l], state_C[l], state_n[l], state_m[l], ts, *wl)
        conv_s.append(cv.astype(state_conv.dtype))
        C_s.append(C.astype(state_C.dtype))
        n_s.append(n.astype(state_n.dtype))
        m_s.append(m.astype(state_m.dtype))
    y_prompt = _rmsnorm(yp, final_norm)
    y_sample = _rmsnorm(ys, final_norm)
    return (y_prompt, y_sample, jnp.stack(conv_p), jnp.stack(C_p), jnp.stack(n_p), jnp.stack(m_p),
            jnp.stack(conv_s), jnp.stack(C_s), jnp.stack(n_s), jnp.stack(m_s))


_drawn_inputs = setup_inputs


def setup_inputs(seed=0):
    import zlib

    import numpy as np

    out = dict(_drawn_inputs(seed))
    spreads = {}
    factors = {'norm_ffn1': 8.0,
     'b_dw': 8.0,
     'ln_conv_g': 200.0,
     'ln_conv_b': 200.0,
     'mh_norm': 200.0,
     'norm_ffn2': 22.686,
     'final_norm': 23.946}
    for name, (base, spread) in spreads.items():
        noise = np.random.default_rng([zlib.crc32(name.encode()), seed]).standard_normal(out[name].shape)
        drawn = base * np.exp(spread * noise) if base else spread * noise
        out[name] = __import__('jax').numpy.asarray(drawn.astype(out[name].dtype))
    for name, factor in factors.items():
        out[name] = (out[name] * factor).astype(out[name].dtype)
    return out
```

```python
from contextlib import ExitStack, contextmanager

import numpy as np
import concourse.bass as bass
from concourse import mybir
from concourse.alu_op_type import AluOpType as ALU

ACT = mybir.ActivationFunctionType
F32 = mybir.dt.float32
F32R = mybir.dt.float32r

P = 128
D = 1024
KT = D // P
NP = 1024
NB, TB = 8, 8
NT = NP + NB * TB
GW = 364
GROUPS = [(0, GW), (GW, 2 * GW), (2 * GW, NT)]
W = 3 * GW
LP = NP - 2 * GW
FF = 2816
FT = FF // P
FG = FT // 2
NV = 9
CW = 31
PAST = CW - 1
H = 4
HD = D // H
CH = 128
NC = NP // CH
C1 = HD + 1
NMOD = 9
EPS = 1e-6
MASKED = -1e30
AB = 4
JOBS_FFN = 2 * FT + 8 * FG
JOBS_BEFORE_TAIL = 1 + JOBS_FFN + 1 + 1 + 8 * KT
MEANS_AFTER = (1, 4)
N_UNITS = 2 * (2 * FT + 2 * FG) + 8 * KT + 3 * KT


class Tally:

    def __init__(self, n=0):
        self.n, self.turn, self.per = n, None, 0

    def __call__(self, more=0):
        n = self.n + more
        return n if self.turn is None else self.turn * self.per + n

    def add(self, k=1):
        self.n += k
        return self()


@contextmanager
def repeat(eng, times, *tallies):
    start = [t.n for t, _ in tallies]
    with eng.Fori(0, times) as turn:
        for t, per in tallies:
            t.turn, t.per = turn, per
        yield turn
        for (t, per), n in zip(tallies, start):
            assert t.n - n == per, (t.n - n, per)
    for (t, per), n in zip(tallies, start):
        t.turn, t.n = None, n + per * times


class Jobs:

    def __init__(self):
        self.job, self.unit, self.part = Tally(), Tally(), Tally()

    def slot(self):
        return self.job.n % 2

    def used(self, more=0):
        t = self.job
        n = (t.n + more) // 2
        return n if t.turn is None else t.turn * (t.per // 2) + n

    def _take(self, tally):
        tally.add()
        s, freed = self.slot(), self.used()
        self.job.add()
        return s, tally(), freed + 1

    def take_unit(self):
        return self._take(self.unit)

    def take_part(self):
        return self._take(self.part)

    def per(self, jobs, units, parts):
        return (self.job, jobs), (self.unit, units), (self.part, parts)


def trunk(nc, t_in, t_out):
    with ExitStack() as ctx:
        at = [(nc.sbuf_base + 63) // 64 * 64]

        def region(nbytes):
            start = at[0]
            at[0] += (nbytes + 31) // 32 * 32
            assert at[0] <= nc.sbuf_usable_end, (at[0], nc.sbuf_usable_end)
            return start

        def place(name, shape, dt, offset):
            return nc.alloc_sbuf_tensor_at(name, shape, dt, offset=offset)

        def own(name, shape, dt=F32):
            return place(name, shape, dt, region(int(np.prod(shape[1:])) * 4))

        TILE = W * 4
        w_raw = own("w_raw", [P, 2, D])
        w_hi = own("w_hi", [P, 2, D], F32R)
        w_lo = own("w_lo", [P, 2, D], F32R)
        u_hi = own("u_hi", [P, KT, W], F32R)
        u_lo = own("u_lo", [P, KT, W], F32R)
        r_x = region(KT * TILE)
        x = place("x", [P, KT, W], F32, r_x)
        qkvo = place("qkvo", [P, 8, W], F32, r_x)
        a_hi = place("a_hi", [P, KT, W], F32R, r_x)
        a_tmp = place("a_tmp", [P, KT, W], F32, r_x)
        r_y = region(KT * TILE)
        y = place("y", [P, KT, W], F32, r_y)
        a_lo = place("a_lo", [P, KT, W], F32R, r_y)
        work = place("work", [P, KT, W], F32, r_y)
        sg, prod, ss, rstd = (work[:, i] for i in (0, 1, 2, 3))
        sq = [work[:, 4], work[:, 5]]
        tn = [work[:, 6], work[:, 7]]
        r_s = region(4 * TILE)
        ada = place("ada", [P, AB, D], F32, r_s)
        b_cur = place("b_cur", [P, 2, W], F32, r_s)
        th = place("th", [P, 2, W], F32, r_s + 2 * TILE)
        r_z = at[0]
        glu = own("glu", [P, 2, PAST + NP])
        glus = own("glus", [P, 2, NB, PAST + TB])
        st = own("st", [P, 3, 2, C1])
        c_cur = own("c_cur", [P, 2, C1])
        ktok = own("ktok", [P, HD])
        vaug = own("vaug", [P, C1])
        vws = own("vws", [P, C1])
        dw = own("dw", [P, P])
        pw = own("pw", [P, P])
        tin = own("tin", [P, C1])
        hn = own("hn", [P, C1])
        hs_of = {kind: own(f"hs_{kind}", [P, HD]) for kind in "ps"}
        g_row = own("g_row", [4, NT])
        g_cur = own("g_cur", [4, NT])
        if at[0] < r_z + KT * TILE:
            region(r_z + KT * TILE - at[0])
        z = place("z", [P, KT, W], F32, r_z)
        hid_hi = place("hid_hi", [P, 2, W], F32R, r_z)
        hid_lo = place("hid_lo", [P, 2, W], F32R, r_z + 2 * TILE)
        mods = own("mods", [P, NMOD * KT, NV])
        m_a = own("m_a", [P, 3, KT, NV])
        m_g = own("m_g", [P, 3, KT, NV])
        xs_tmp = own("xs_tmp", [P, NB * TB])
        b_ada = own("b_ada", [P, NMOD * KT])
        b_in = own("b_in", [P, H, 16])
        vecs = own("vecs", [P, 8, KT])
        w_dw = own("w_dw", [P, KT, CW])
        dw_cur = own("dw_cur", [P, 2, CW])
        cs = own("cs", [P, KT, NV])
        col = own("col", [P, NC, 16])
        cols = own("cols", [TB, NB, 16])
        col_h = own("col_h", [P, NC, 4])
        cols_h = own("cols_h", [TB, NB, 4])
        ap_h = own("ap_h", [P, NC + NB])
        apv = own("apv", [4, NC + NB])
        apm = own("apm", [4, NC + NB])
        small = own("small", [P, 8])
        ident = own("ident", [P, P])
        mask = own("mask", [P, P])
        mean = own("mean", [P, P])
        ones = own("ones", [4, P])
        eps = own("eps", [P, 1])
        one = own("one", [P, 1])
        b_if = own("b_if", [P, 1])
        mc = own("mc", [4, NC + 1])
        ms = own("ms", [4, NB])
        m_fin = own("m_fin", [4, 1 + NB])
        wg_hi = place("wg_hi", [P, KT, 36], F32R, r_z)
        wg_lo = place("wg_lo", [P, KT, 36], F32R, r_z + KT * 36 * 4)
        wg_raw = place("wg_raw", [P, KT, 36], F32, r_z + 2 * KT * 36 * 4)
        rows = place("rows", [P, KT, W], F32, r_y)
        NORM1, NORM2, NORM3, NORMF, B_DW, LN_G, LN_B, MH = range(8)
        ROW_I, ROW_Z, ROW_E, ROW_1, ROW_B, ROW_T, ROW_Q = range(7)

        slots = ctx.enter_context(nc.psum_tensor("slots", [P, 2, 3, 512], F32))
        bank_x = ctx.enter_context(nc.psum_tensor("bank_x", [P, 512], F32))
        bank_y = ctx.enter_context(nc.psum_tensor("bank_y", [P, 512], F32))

        x_keep = nc.dram_tensor("x_keep", (P, KT, W), F32, kind="Internal").ap()
        b_keep = nc.dram_tensor("b_keep", (H, P, 2, W), F32, kind="Internal").ap()
        ga_keep = nc.dram_tensor("ga_keep", (KT, P, W), F32, kind="Internal").ap()
        gb_keep = nc.dram_tensor("gb_keep", (KT, P, W), F32, kind="Internal").ap()

        def sem(name):
            return ctx.enter_context(nc.semaphore(name))

        x_in, c_in, consts_in, gate_w_in = (sem(n) for n in ("x_in", "c_in", "consts_in", "gate_w_in"))
        w_in = [sem(f"w_in{i}") for i in range(2)]
        ada_in = [sem(f"ada_in{i}") for i in range(AB)]
        w_split, unit_done, part_done = sem("w_split"), sem("unit_done"), sem("part_done")
        w_hi_done = sem("w_hi_done")
        slot_free = [sem("slot_free0"), sem("slot_free1")]
        tables = sem("tables")
        x_padded, consts_ready, biases_ready, wg_cleared = (sem(n) for n in ("x_padded", "consts_ready", "biases_ready", "wg_cleared"))
        cs_ready, ada_used, ada_free = sem("cs_ready"), sem("ada_used"), sem("ada_free")
        sq_done, sq_added, t_ready, hi_ready, h_ready = (sem(n) for n in ("sq_done", "sq_added", "t_ready", "hi_ready", "h_ready"))
        x_final = sem("x_final")
        hid_hi_done, hid_ready = sem("hid_hi_done"), sem("hid_ready")
        x_out, x_back = sem("x_out"), [sem(f"x_back{k}") for k in range(KT)]
        wg_ready, rows_act, rows_dve, cols_ready = sem("wg_ready"), sem("rows_act"), sem("rows_dve"), sem("cols_ready")
        x_full, x_free, y_full, y_free = sem("x_full"), sem("x_free"), sem("y_full"), sem("y_free")
        head_ready, d_ready, rd_ready, r_ready, hs_ready = (sem(n) for n in ("head_ready", "d_ready", "rd_ready", "r_ready", "hs_ready"))
        st_in, st_out = [sem(f"st_in{i}") for i in range(3)], [sem(f"st_out{i}") for i in range(3)]
        c_out, m_out, b_out = sem("c_out"), sem("m_out"), sem("b_out")
        m_ready = sem("m_ready")
        th_out = [sem("th_out0"), sem("th_out1")]
        taps_done, glus_in, conv_out = sem("taps_done"), sem("glus_in"), [sem("conv_out0"), sem("conv_out1")]
        b_back = [sem("b_back0"), sem("b_back1")]
        g_back = [sem("g_back0"), sem("g_back1")]
        b_hi_done, b_ready = sem("b_hi_done"), sem("b_ready")
        y_cent, ysq_done, ysq_added, y_norm, a_hi_done, a_ready = (
            sem(n) for n in ("y_cent", "ysq_done", "ysq_added", "y_norm", "a_hi_done", "a_ready"))
        z_done, z_hi_done, z_ready = sem("z_done"), sem("z_hi_done"), sem("z_ready")
        out_ready, out_done = sem("out_ready"), [sem(f"out_done{i}") for i in range(4)]

        def bank3(s):
            return slots[:, s, :, 0:GW]

        def tile3(ap):
            return ap.rearrange("p (g n) -> p g n", g=3)

        def per_batch(ap8, k=None):
            return ap8.unsqueeze(2).to_broadcast([P, NB, TB])

        def sample3(ap64):
            return ap64.rearrange("p (b t) -> p b t", b=NB)

        def pieces():
            out = []
            for i in range(NC):
                out += [("p", i, 0), ("p", i, 1), ("p", i, 2), ("s", i - 1, 3),
                        ("s", i, 0), ("s", i, 1), ("s", i, 2), ("p", i, 3)]
            return out
        PIECES = pieces()

        def seg(kind, i):
            return (i * CH, CH) if kind == "p" else (NP + i * TB, TB)

        def bias_of(h, j):
            return b_in[:, h, j:j + 1] if isinstance(h, int) else b_in[:, bass.ds(h, 1), j:j + 1].rearrange("p a b -> p (a b)")

        def at_tile(t, n, merge):
            return t[n] if isinstance(n, int) else t[bass.ds(n, 1)].rearrange(merge)

        block = ctx.enter_context(nc.Block())

        @block.sync
        def _(sp):
            unit, batch = Tally(), Tally()

            def load_unit():
                slot = unit.n % 2
                if unit.n >= 2:
                    sp.wait_ge(w_split, unit(-1))
                n = unit()
                src = t_in["w_units"][n] if unit.turn is None else t_in["w_units"][bass.ds(n, 1)].rearrange("o p n -> p (o n)")
                sp.dma_start(w_raw[:, slot, :], src).then_inc(w_in[slot], 16)
                unit.add()

            def load_ada():
                for j in range(AB):
                    if batch.n >= 1:
                        sp.wait_ge(ada_used, (batch() - 1) * AB + j + 1)
                    n = batch() * AB + j
                    src = t_in["ada_units"][n] if batch.turn is None else t_in["ada_units"][bass.ds(n, 1)].rearrange("o p n -> p (o n)")
                    sp.dma_start(ada[:, j, :], src).then_inc(ada_in[j], 16)
                batch.add()

            sp.dma_start(cs[:], t_in["c"]).then_inc(c_in, 16)
            load_ada()
            sp.dma_start(x[:, :, 0:NP], t_in["x_prompt"]).then_inc(x_in, 16)
            sp.dma_start(x[:, :, NP:NT], t_in["x_sample"]).then_inc(x_in, 16)
            for dst, name in ((b_ada, "b_ada"), (b_in, "b_in"), (vecs, "vecs"), (w_dw, "w_dw")):
                sp.dma_start(dst[:], t_in[name]).then_inc(consts_in, 16)
            sp.dma_start(b_if[0:4, :], t_in["b_i"]).then_inc(consts_in, 16)
            sp.dma_start(b_if[32:36, :], t_in["b_f"]).then_inc(consts_in, 16)
            sp.dma_start(ms[:], t_in["state_m"]).then_inc(consts_in, 16)
            for _ in range(3):
                load_ada()
            load_unit()
            load_unit()
            for _ in range(4):
                load_ada()
                if unit.n < 4:
                    load_unit()
            with repeat(sp, FG - 1, (unit, 6), (batch, 1)):
                for _ in range(3):
                    load_unit()
                load_ada()
                for _ in range(3):
                    load_unit()
            load_unit()
            load_unit()
            load_unit()
            load_unit()
            sp.wait_ge(x_final, KT)
            sp.dma_start(x_keep, x[:]).then_inc(x_out, 16)
            for t in range(2):
                sp.dma_start(glus[:, t, :, 0:PAST], t_in["state_conv"][t]).then_inc(glus_in, 16)
            sp.wait_ge(wg_cleared, 1)
            sp.dma_start(wg_raw[:, :, 0:4], t_in["w_if"][:, :, 0:4]).then_inc(gate_w_in, 16)
            sp.dma_start(wg_raw[:, :, 32:36], t_in["w_if"][:, :, 4:8]).then_inc(gate_w_in, 16)
            for _ in range(2):
                load_unit()
            with repeat(sp, H - 1, (unit, 16)):
                for _ in range(16):
                    load_unit()
            for _ in range(12):
                load_unit()
            tail = Jobs()
            tail.job.n = JOBS_BEFORE_TAIL
            reads = []
            for m in range(KT):
                reads.append(tail.take_unit()[::2])
                if m in MEANS_AFTER:
                    tail.take_part()

            def load_gate(n):
                src = (gb_keep if n < KT else ga_keep)[n % KT]
                if n >= 2:
                    if n - 2 < KT:
                        sp.wait_ge(slot_free[reads[n - 2][0]], reads[n - 2][1])
                    else:
                        sp.wait_ge(z_done, n - 1 - KT)
                sp.dma_start(th[:, n % 2, :], src).then_inc(g_back[n % 2], 16)

            load_unit()
            load_unit()
            sp.wait_ge(b_out, 16 * (H + 1))
            for k in range(KT):
                if k >= 2:
                    sp.wait_ge(b_ready, k - 1)
                sp.dma_start(b_cur[:, k % 2, :], b_keep[k // 2, :, k % 2, :]).then_inc(b_back[k % 2], 16)
            for s in range(2):
                sp.wait_ge(th_out[s], 16 * (KT + 1))
            load_gate(0)
            load_gate(1)
            for n in range(2 * KT):
                load_unit()
                if n + 2 < 2 * KT:
                    load_gate(n + 2)
            sp.wait_ge(unit_done, unit.n - 2)
            for k in range(KT):
                sp.dma_start(x[:, k, :], x_keep[:, k, :]).then_inc(x_back[k], 16)
            for _ in range(KT - 2):
                load_unit()
            for _ in range(4):
                load_unit()
            with repeat(sp, FG - 1, (unit, 6)):
                for _ in range(6):
                    load_unit()
            load_unit()
            load_unit()
            assert unit.n == N_UNITS, (unit.n, N_UNITS)
            for k in range(KT):
                sp.wait_ge(out_ready, k + 1)
                sp.dma_start(t_out["y"][k], work[:, 4 + k % 4, 0:NT]).then_inc(out_done[k % 4], 16)
            for n in range(4):
                sp.wait_ge(out_done[n], 16 * KT // 4)
            for t in range(2):
                sp.wait_ge(conv_out[t], 16 * KT)
            sp.wait_ge(m_out, 16)

        @block.gpsimd
        def _(pool):
            unit = Tally()
            pool.memset(ident[:], 0.0).then_inc(tables, 1)
            pool.memset(mask[:], 0.0).then_inc(tables, 1)
            pool.memset(one[:], 1.0).then_inc(tables, 1)
            pool.wait_ge(tables, 3)
            pool.affine_select(out=ident[:], in_=ident[:], compare_op=ALU.not_equal, fill=1.0, base=0,
                               pattern=[[-1, P]], channel_multiplier=1).then_inc(tables, 1)
            pool.affine_select(out=mask[:], in_=mask[:], compare_op=ALU.is_ge, fill=MASKED, base=0,
                               pattern=[[1, P]], channel_multiplier=-1).then_inc(tables, 1)

            def split(slot, first):
                pool.wait_ge(w_in[slot], (unit() - slot) * 8 + 16)
                if not first:
                    pool.wait_ge(unit_done, unit(-1))
                pool.tensor_tensor(w_hi[:, slot, :], w_raw[:, slot, :], one[:].to_broadcast([P, D]), ALU.mult).then_inc(w_hi_done, 1)
                pool.wait_ge(w_hi_done, unit(1))
                pool.tensor_tensor(w_lo[:, slot, :], w_raw[:, slot, :], w_hi[:, slot, :].bitcast(F32),
                                   ALU.subtract).then_inc(w_split, 1)
                unit.add()

            split(0, True)
            split(1, True)
            with repeat(pool, N_UNITS // 2 - 1, (unit, 2)):
                split(0, False)
                split(1, False)

        @block.tensor
        def _(pe):
            jobs, batch = Jobs(), Tally()
            hid = Tally()
            xu, yu = Tally(), Tally()
            steps, heads = Tally(), Tally()
            sts = [Tally() for _ in range(3)]

            def open_slot():
                s = jobs.slot()
                if jobs.job.n >= 2:
                    pe.wait_ge(slot_free[s], jobs.used())
                return s

            def three_passes(s, w_of, hi, lo, k, K):
                for q, (w, r) in enumerate(((w_hi, hi), (w_hi, lo), (w_lo, hi))):
                    for g, (a, b) in enumerate(GROUPS):
                        last = pe.matmul(slots[:, s, g, 0:b - a], w_of(w), r[:, k, a:b],
                                         start=(k == 0 and q == 0), stop=(k == K - 1 and q == 2))
                return last

            def project(hi, lo, ready=None, base=0, between=None):
                s = open_slot()
                u = jobs.unit.n % 2
                pe.wait_ge(w_split, jobs.unit(1))
                for k in range(KT):
                    if ready is not None:
                        pe.wait_ge(ready, base + k + 1)
                    last = three_passes(s, lambda w: w[:, u, k * P:(k + 1) * P], hi, lo, k, KT)
                    if k == KT - 1:
                        last.then_inc(unit_done, 1)
                    if between:
                        between(k)
                jobs.take_unit()

            def down():
                pe.wait_ge(hid_ready, hid())
                for half in range(2):
                    u = jobs.unit.n % 2
                    pe.wait_ge(w_split, jobs.unit(1))
                    for m in range(4):
                        s = open_slot()
                        for k in range(2):
                            last = three_passes(s, lambda w: w[:, u, k * 512 + m * P:k * 512 + (m + 1) * P],
                                                hid_hi, hid_lo, k, 2)
                        if m < 3:
                            last.then_inc(part_done, 1)
                            jobs.take_part()
                        else:
                            last.then_inc(unit_done, 1)
                            jobs.take_unit()

            def modulate(bank):
                if batch.turn is not None or batch.n >= 2:
                    same = 1 if batch.turn is None and bank != "last" else 0
                    pe.wait_ge(ada_free, batch(-same))
                b = bank_y if bank == "y" else bank_x
                for j in range(AB):
                    pe.wait_ge(ada_in[j], (batch() + 1) * 16)
                    for k in range(KT):
                        last = pe.matmul(b[:, 16 * j:16 * j + NV], ada[:, j, k * P:(k + 1) * P], cs[:, k, :],
                                         start=(k == 0), stop=(k == KT - 1))
                    last.then_inc(ada_used, 1)
                batch.add()

            def reduce_features(src, ready, value):
                s = open_slot()
                pe.wait_ge(ready, value)
                for g, (a, b) in enumerate(GROUPS):
                    last = pe.matmul(slots[:, s, g, 0:b - a], mean[:], src[:, a:b], start=True, stop=True)
                last.then_inc(part_done, 1)
                jobs.take_part()

            def ffn(p, ada_too):
                for n in range(4):
                    project(u_hi, u_lo, h_ready if n == 0 else None, p * KT)
                    if ada_too:
                        modulate("xy"[n % 2])
                hid.add(2)
                extra = [(batch, 1)] if ada_too else []
                with repeat(pe, FG - 1, *jobs.per(12, 6, 6), (hid, 2), *extra):
                    project(u_hi, u_lo)
                    project(u_hi, u_lo)
                    down()
                    hid.add(2)
                    project(u_hi, u_lo)
                    project(u_hi, u_lo)
                    if ada_too:
                        modulate("x")
                down()

            pe.wait_ge(cs_ready, 1)
            for n in range(4):
                modulate("xy"[n % 2])
            pe.wait_ge(consts_ready, 1)
            reduce_features(ss, sq_added, KT)
            ffn(0, True)

            reduce_features(ss, sq_added, 2 * KT)
            s = open_slot()
            pe.wait_ge(wg_ready, 1)
            for k in range(KT):
                pe.wait_ge(h_ready, KT + k + 1)
                for q, (w, r) in enumerate(((wg_hi, u_hi), (wg_hi, u_lo), (wg_lo, u_hi))):
                    for g, (a, b) in enumerate(GROUPS):
                        last = pe.matmul(slots[0:36, s, g, 0:b - a], w[:, k, :], r[:, k, a:b],
                                         start=(k == 0 and q == 0), stop=(k == KT - 1 and q == 2))
            last.then_inc(part_done, 1)
            jobs.take_part()
            for _ in range(4):
                project(u_hi, u_lo)
            pe.wait_ge(rows_dve, 4)
            pe.wait_ge(rows_act, 4)
            pe.wait_ge(ada_free, batch.n)
            pe.wait_ge(tables, 5)
            for n in range(4):
                bank, full, free, use = ((bank_x, x_full, x_free, xu), (bank_y, y_full, y_free, yu))[n % 2]
                if n >= 2:
                    pe.wait_ge(free, use())
                for j in range(4):
                    if n < 2:
                        c = 4 * n + j
                        last = pe.transpose(bank[:, j * P:(j + 1) * P], rows[:, ROW_Q, c * CH:(c + 1) * CH], ident[:])
                    else:
                        a = NP + (4 * (n - 2) + j) * TB
                        last = pe.matmul(bank[0:TB, j * P:(j + 1) * P], rows[:, ROW_Q, a:a + TB], ident[:],
                                         start=True, stop=True)
                last.then_inc(full, 1)
                use.add()

            q_of = lambda m, a, n: qkvo[:, m, a:a + n]
            k_of = lambda m, a, n: qkvo[:, 2 + m, a:a + n]
            v_of = lambda m, a, n: qkvo[:, 4 + m, a:a + n]

            def piece(kind, i, stage):
                if i < 0:
                    return
                a, L = seg(kind, i)
                mem = c_cur if kind == "p" else st[:, i % 3]
                pe.wait_ge(x_free, xu())
                if stage == 0:
                    for n, src in enumerate((k_of(0, a, L), k_of(1, a, L), v_of(0, a, L), v_of(1, a, L))):
                        if kind == "p":
                            last = pe.transpose(bank_x[0:L, n * P:(n + 1) * P], src, ident[:])
                        else:
                            last = pe.matmul(bank_x[0:L, n * P:(n + 1) * P], src, ident[:], start=True, stop=True)
                    last.then_inc(x_full, 1)
                    pe.wait_ge(y_free, yu())
                    for m in range(2):
                        pe.matmul(bank_y[0:L, 0:L], k_of(m, a, L), q_of(m, a, L), start=(m == 0), stop=(m == 1))
                    pe.matmul(bank_y[0:L, P:P + L], ones[:, 0:L], g_cur[:, a:a + L], start=True, stop=False)
                    pe.matmul(bank_y[0:L, P:P + L], ident[0:L, 0:L], mask[0:L, 0:L], start=False, stop=True).then_inc(y_full, 1)
                elif stage == 1:
                    if kind == "s":
                        pe.wait_ge(st_in[i % 3], 16 * sts[i % 3](1))
                        sts[i % 3].add()
                    if kind == "s":
                        pe.wait_ge(y_free, yu())
                    for m in range(2):
                        last = pe.matmul(bank_x[0:L, 0:C1], q_of(m, a, L), mem[:, m, :], start=(m == 0), stop=(m == 1))
                    last.then_inc(x_full, 1)
                    if kind == "p":
                        pe.wait_ge(y_free, yu())
                    pe.matmul(bank_y[0:L, 0:C1], pw[0:L, 0:L], vaug[0:L, :], start=True, stop=True).then_inc(y_full, 1)
                elif stage == 2:
                    pe.matmul(bank_x[:, 0:C1], ktok[0:L, 0:P], vws[0:L, :], start=True, stop=True).then_inc(x_full, 1)
                    pe.wait_ge(y_free, yu())
                    pe.matmul(bank_y[:, 0:C1], ktok[0:L, P:HD], vws[0:L, :], start=True, stop=True).then_inc(y_full, 1)
                else:
                    pe.wait_ge(hs_ready, steps.add())
                    for m in range(2):
                        src, dst = hs_of[kind][0:L, m * P:(m + 1) * P], bank_x[:, m * P:m * P + L]
                        if kind == "p":
                            last = pe.transpose(dst, src, ident[:])
                        else:
                            last = pe.matmul(dst, src, ident[0:L, 0:L], start=True, stop=True)
                    last.then_inc(x_full, 1)
                xu.add()
                if stage < 3:
                    yu.add()

            def section_a():
                for _ in range(8):
                    project(u_hi, u_lo)

            def section_b(n_units):
                s = jobs.slot()
                for more in (0, 1):
                    pe.wait_ge(slot_free[(s + more) % 2], jobs.used(more))
                pe.wait_ge(head_ready, heads.add())
                pe.wait_ge(x_free, xu())
                pe.matmul(bank_x[:, 0:NC + NB], ones[:], apm[:], start=True, stop=True).then_inc(x_full, 1)
                xu.add()
                each = len(PIECES) // (KT * n_units)
                for n in range(n_units):
                    def between(k):
                        for i in range(each):
                            piece(*PIECES[(n * KT + k) * each + i])
                    project(u_hi, u_lo, between=between)
                piece("s", NB - 1, 3)

            sx = [(sts[0], 3), (sts[1], 3), (sts[2], 2)]
            with repeat(pe, H - 1, *jobs.per(16, 16, 0), (xu, 65), (yu, 48), (steps, 16), (heads, 1), *sx):
                section_a()
                section_b(8)
            section_a()
            section_b(4)

            for m in range(KT):
                project(u_hi, u_lo, b_ready if m == 0 else None)
                if m == MEANS_AFTER[0]:
                    reduce_features(a_tmp[:, 5], y_cent, 1)
                if m == MEANS_AFTER[1]:
                    reduce_features(b_cur[:, 0], ysq_added, KT)
            for m in range(KT):
                project(a_hi, a_lo, a_ready if m == 0 else None)
            for m in range(KT):
                project(u_hi, u_lo, z_ready if m == 0 else None)
            reduce_features(ss, sq_added, 3 * KT)
            ffn(2, False)
            reduce_features(ss, sq_added, 4 * KT)

        @block.scalar
        def _(act):
            jobs = Jobs()
            sqs = Tally()
            xu, yu = Tally(), Tally()
            steps = Tally()
            outs = [Tally(1), Tally(1)]
            taps = Tally()
            stores = [Tally(1) for _ in range(3)]

            def squares(p):
                for k in range(KT):
                    if p > 0:
                        act.wait_ge(x_final, (p - 1) * KT + k + 1)
                    elif k == 0:
                        act.wait_ge(x_in, 32)
                    if sqs.n >= 2:
                        act.wait_ge(sq_added, sqs(-1))
                    act.activation(sq[k % 2][:, 0:NT], x[:, k, 0:NT], ACT.Square).then_inc(sq_done, 1)
                    sqs.add()

            def root(dst):
                s, done, _ = jobs.take_part()
                act.wait_ge(part_done, done)
                act.activation(tile3(dst), bank3(s), ACT.Sqrt, bias=eps[:, 0:1]).then_inc(slot_free[s], 1)

            def norm(p):
                squares(p)
                root(rstd)
                sh = mods[:, 3 * p * KT:(3 * p + 1) * KT, :]
                for k in range(KT):
                    act.wait_ge(t_ready, p * KT + k + 1)
                    act.activation(u_hi[:, k, 0:NP], tn[k % 2][:, 0:NP], ACT.Identity, bias=sh[:, k, 0:1])
                    act.activation(u_hi[:, k, NP:NT], tn[k % 2][:, NP:NT], ACT.Copy).then_inc(hi_ready, 1)

            def ffn():
                def gate():
                    s, done, _ = jobs.take_unit()
                    act.wait_ge(unit_done, done)
                    act.activation(tile3(sg), bank3(s), ACT.Silu).then_inc(slot_free[s], 1)

                def high(j, up):
                    act.wait_ge(slot_free[up[0]], up[2])
                    act.activation(hid_hi[:, j, :], prod, ACT.Copy).then_inc(hid_hi_done, 1)

                for j in range(2):
                    gate()
                    high(j, jobs.take_unit())
                with repeat(act, FG - 1, *jobs.per(12, 6, 6)):
                    gate()
                    up = jobs.take_unit()
                    for _ in range(2):
                        for _ in range(3):
                            jobs.take_part()
                        _, done, _ = jobs.take_unit()
                    act.wait_ge(unit_done, done)
                    high(0, up)
                    gate()
                    high(1, jobs.take_unit())
                for _ in range(2):
                    for _ in range(3):
                        jobs.take_part()
                    jobs.take_unit()

            act.wait_ge(c_in, 16)
            act.activation(cs[:], cs[:], ACT.Silu).then_inc(cs_ready, 1)
            act.wait_ge(consts_ready, 1)
            norm(0)
            ffn()
            norm(1)

            act.wait_ge(consts_in, 16 * 7)
            s, done, _ = jobs.take_part()
            act.wait_ge(part_done, done)
            act.wait_ge(rows_dve, 1)
            act.activation(tile3(rows[0:4, ROW_I, :]), slots[0:4, s, :, 0:GW], ACT.Identity, bias=b_if[0:4, 0:1])
            act.activation(tile3(rows[0:4, ROW_Z, :]), slots[32:36, s, :, 0:GW], ACT.Identity,
                           bias=b_if[32:36, 0:1]).then_inc(slot_free[s], 1)
            act.drain()
            act.activation(rows[0:4, ROW_E, :], rows[0:4, ROW_Z, :], ACT.Abs)
            act.drain()
            act.activation(rows[0:4, ROW_E, :], rows[0:4, ROW_E, :], ACT.Exp, scale=-1.0)
            act.drain()
            act.activation(rows[0:4, ROW_E, :], rows[0:4, ROW_E, :], ACT.Ln, bias=1.0).then_inc(rows_act, 1)

            def gate_tile(n, bias):
                s, done, _ = jobs.take_unit()
                act.wait_ge(unit_done, done)
                act.activation(tile3(n), bank3(s), ACT.Tanh, bias=bias, scale=0.5).then_inc(slot_free[s], 1)

            def rows_to_exp():
                act.wait_ge(rows_dve, 2)
                act.activation(rows[32:36, ROW_Q, 0:NT], rows[0:4, ROW_I, 0:NT], ACT.Exp).then_inc(rows_act, 1)
                act.activation(rows[64:68, ROW_Q, 0:NT], rows[0:4, ROW_Z, 0:NT], ACT.Exp, scale=-1.0).then_inc(rows_act, 1)
                act.wait_ge(rows_dve, 3)
                act.activation(rows[96:100, ROW_Q, 0:NT], rows[0:4, ROW_T, 0:NT], ACT.Exp).then_inc(rows_act, 1)
                act.wait_ge(m_ready, 1)
                act.dma_start(t_out["m"], m_fin[:]).then_inc(m_out, 16)

            rows_to_exp()

            def conv_gate(h1, t):
                if outs[t].turn is not None:
                    act.wait_ge(th_out[t], 16 * outs[t]())
                gate_tile(th[:, t, :], bias_of(h1, 8 + 2 * t))

            def conv_stores(h1, t):
                s, _, freed = jobs.take_unit()
                act.wait_ge(slot_free[s], freed)
                act.dma_start(at_tile(t_out["conv_p"], 2 * h1 + t, "o p n -> p (o n)"),
                              glu[:, t, NP:NP + PAST]).then_inc(conv_out[t], 16)
                act.dma_start(at_tile(t_out["conv_s"], 2 * h1 + t, "o p b n -> p (o b) n"),
                              glus[:, t, :, TB:TB + PAST]).then_inc(conv_out[t], 16)

            act.wait_ge(biases_ready, 1)
            for t in range(2):
                conv_gate(0, t)
                conv_stores(0, t)

            def section_a(h):
                for j in range(8):
                    if j >= 6:
                        gate_tile(qkvo[:, j, :], bias_of(h, j))
                        continue
                    s, done, _ = jobs.take_unit()
                    act.wait_ge(unit_done, done)
                    act.activation(tile3(qkvo[:, j, :]), bank3(s), ACT.Identity, bias=bias_of(h, j),
                                   scale=HD ** -0.5 if j < 2 else 1.0).then_inc(slot_free[s], 1)

            def st_dram(t, h, b):
                return t[h, b] if isinstance(h, int) else t[bass.ds(h, 1), b].rearrange("o p m c -> p (o m) c")

            def load_state(h, b):
                n = b % 3
                act.wait_ge(st_out[n], 16 * stores[n]())
                act.dma_start(st[:, n], st_dram(t_in["state"], h, b)).then_inc(st_in[n], 16)

            def piece(h, kind, i, stage):
                if i < 0:
                    return
                _, L = seg(kind, i)
                c = col_h[:, i, :] if kind == "p" else cols_h[:, i, :]
                if stage == 0:
                    act.wait_ge(x_full, xu.add())
                    act.activation(ktok[0:L, :], bank_x[0:L, 0:HD], ACT.Copy)
                    act.activation(vaug[0:L, 0:HD], bank_x[0:L, HD:2 * HD], ACT.Copy)
                    act.activation(vws[0:L, 0:HD], bank_x[0:L, HD:2 * HD], ACT.Copy, scale=c[0:L, 3:4]).then_inc(x_free, 1)
                    act.wait_ge(y_full, yu.add())
                    act.activation(dw[0:L, 0:L], bank_y[0:L, P:P + L], ACT.Exp, bias=c[0:L, 0:1]).then_inc(d_ready, 1)
                elif stage == 1:
                    act.wait_ge(x_full, xu.add())
                    act.activation(tin[0:L, :], bank_x[0:L, 0:C1], ACT.Copy, scale=c[0:L, 1:2]).then_inc(x_free, 1)
                    yu.add()
                elif stage == 2:
                    act.wait_ge(rd_ready, steps.add())
                    act.activation(tin[0:L, 0:HD], hn[0:L, 0:HD], ACT.Square, scale=small[0:L, 0:1],
                                   accum_out=small[0:L, 1:2])
                    act.drain()
                    act.activation(small[0:L, 2:3], small[0:L, 1:2], ACT.Sqrt, bias=eps[0:L, 0:1],
                                   scale=1.0 / HD).then_inc(r_ready, 1)
                    xu.add()
                    yu.add()
                    if kind == "s":
                        act.wait_ge(y_free, yu())
                        act.dma_start(st_dram(t_out["C_s"], h, i), st[:, i % 3]).then_inc(st_out[i % 3], 16)
                        stores[i % 3].add()
                        if i + 2 < NB:
                            load_state(h, i + 2)
                else:
                    xu.add()

            def section_b(h, n_units, last):
                if not last:
                    act.wait_ge(taps_done, taps.add())
                    for t in range(2):
                        act.dma_start(glus[:, t, :, 0:PAST],
                                      t_in["state_conv"][bass.ds(2 * h + 2 + t, 1)].rearrange("o p b n -> p (o b) n")
                                      ).then_inc(glus_in, 16)
                load_state(h, 0)
                load_state(h, 1)
                xu.add()
                each = len(PIECES) // (KT * n_units)
                for n in range(n_units):
                    for q in PIECES[n * KT * each:(n + 1) * KT * each]:
                        piece(h, *q)
                    if n_units == 8 and n < 4:
                        (conv_stores if n % 2 else conv_gate)(h + 1, n // 2)
                        continue
                    j = n - (n_units - 4)
                    t = j % 2
                    act.wait_ge(th_out[t], 16 * outs[t]())
                    gate_tile(th[:, t, :], bias_of(h, 12 + j))
                    dst = at_tile(ga_keep if j < 2 else gb_keep, 2 * h + t, "o p n -> p (o n)")
                    act.drain()
                    act.dma_start(dst, th[:, t, :]).then_inc(th_out[t], 16)
                    outs[t].add()
                piece(h, "s", NB - 1, 3)
                act.wait_ge(x_free, xu())
                act.dma_start(at_tile(b_keep, h, "o p m n -> p (o m) n"), b_cur[:]).then_inc(b_out, 16)
                act.dma_start(at_tile(t_out["C_p"], h, "o p m n -> p (o m) n"), c_cur[:]).then_inc(c_out, 16)

            sx = [(stores[0], 3), (stores[1], 3), (stores[2], 2), (outs[0], 2), (outs[1], 2), (taps, 1)]
            xu.add(2)
            yu.add(2)
            act.wait_ge(x_out, 16)
            with repeat(act, H - 1, *jobs.per(16, 16, 0), (xu, 65), (yu, 48), (steps, 16), *sx) as h:
                section_a(h)
                section_b(h, 8, False)
            section_a(H - 1)
            section_b(H - 1, 4, True)

            for k in range(KT):
                act.wait_ge(b_back[k % 2], 16 * (k // 2 + 1))
                act.activation(u_hi[:, k, :], b_cur[:, k % 2, :], ACT.Copy).then_inc(b_hi_done, 1)
            for k in range(KT):
                act.wait_ge(y_cent, k + 2)
                if k >= 2:
                    act.wait_ge(ysq_added, k - 1)
                act.activation(a_tmp[:, 6 + k % 2, 0:NT], y[:, k, 0:NT], ACT.Square).then_inc(ysq_done, 1)
            for _ in range(2):
                jobs.take_unit()
            jobs.take_part()
            for _ in range(3):
                jobs.take_unit()
            root(b_cur[:, 0, :])
            for k in range(KT):
                act.wait_ge(y_norm, k + 1)
                act.activation(y[:, k, :], y[:, k, :], ACT.Silu, bias=vecs[:, LN_B, k:k + 1],
                               scale=vecs[:, LN_G, k:k + 1])
                act.drain()
                act.activation(a_hi[:, k, :], y[:, k, :], ACT.Copy).then_inc(a_hi_done, 1)
            for _ in range(3):
                jobs.take_unit()
            for k in range(KT):
                jobs.take_unit()
                act.wait_ge(z_done, k + 1)
                act.activation(u_hi[:, k, :], z[:, k, :], ACT.Copy).then_inc(z_hi_done, 1)
            for _ in range(KT):
                jobs.take_unit()
            norm(2)
            ffn()
            squares(3)
            root(rstd)
            for n in range(3):
                act.wait_ge(st_out[n], 16 * stores[n].n)
            act.wait_ge(c_out, 16 * (H + 1))

        @block.vector
        def _(dve):
            jobs = Jobs()
            batch, prods, sqs = Tally(), Tally(), Tally()
            xu, yu, steps, heads = Tally(), Tally(), Tally(), Tally()

            def stt(out, in0, scalar, in1, op0, op1):
                return dve.scalar_tensor_tensor(out=out, in0=in0, scalar=scalar, in1=in1, op0=op0, op1=op1)

            def ada_evac(bank):
                batch.add()
                dve.wait_ge(ada_used, batch() * AB)
                b = (bank_x if bank == "x" else bank_y)[:, 0:16 * AB].rearrange("p (j n) -> p j n", j=AB)[:, :, 0:NV]
                if batch.turn is None:
                    n = (batch.n - 1) * AB
                    dst, bias = mods[:, n:n + AB, :], b_ada[:, n:n + AB]
                else:
                    n = batch(-1) * AB
                    dst, bias = mods[:, bass.ds(n, AB), :], b_ada[:, bass.ds(n, AB)]
                dve.tensor_tensor(dst, b, bias.unsqueeze(2).to_broadcast([P, AB, NV]), ALU.add).then_inc(ada_free, 1)

            def derive_norm(p, gain):
                stt(m_a[:, p], mods[:, (3 * p + 1) * KT:(3 * p + 2) * KT, :], 1.0,
                    vecs[:, gain, :].unsqueeze(2).to_broadcast([P, KT, NV]), ALU.add, ALU.mult)

            def derive_gate(p):
                dve.tensor_scalar(m_g[:, p], mods[:, (3 * p + 2) * KT:(3 * p + 3) * KT, :], 0.5, None, ALU.mult)

            def sum_squares(p):
                for k in range(KT):
                    dve.drain()
                    dve.wait_ge(sq_done, sqs.add())
                    if k == 0:
                        last = dve.tensor_copy(ss[:, 0:NT], sq[0][:, 0:NT])
                    else:
                        last = dve.tensor_tensor(ss[:, 0:NT], ss[:, 0:NT], sq[k % 2][:, 0:NT], ALU.add)
                    last.then_inc(sq_added, 1)
                s, _, freed = jobs.take_part()
                dve.drain()
                dve.wait_ge(slot_free[s], freed)
                dve.reciprocal(rstd[:, 0:NT], rstd[:, 0:NT])
                dve.drain()

            def norm(p):
                sum_squares(p)
                sh = mods[:, 3 * p * KT:(3 * p + 1) * KT, :]

                def scaled(k):
                    t = tn[k % 2]
                    ts = sample3(t[:, NP:NT])
                    dve.drain()
                    dve.tensor_tensor(t[:, NP:NT], x[:, k, NP:NT], rstd[:, NP:NT], ALU.mult)
                    stt(t[:, 0:NP], x[:, k, 0:NP], m_a[:, p, k, 0:1], rstd[:, 0:NP], ALU.mult, ALU.mult)
                    dve.drain()
                    dve.tensor_tensor(ts, ts, per_batch(m_a[:, p, k, 1:NV]), ALU.mult)
                    dve.drain()
                    dve.tensor_tensor(ts, ts, per_batch(sh[:, k, 1:NV]), ALU.add).then_inc(t_ready, 1)

                def low(k):
                    t = tn[k % 2]
                    dve.wait_ge(hi_ready, p * KT + k + 1)
                    stt(u_lo[:, k, 0:NP], t[:, 0:NP], sh[:, k, 0:1], u_hi[:, k, 0:NP].bitcast(F32), ALU.add, ALU.subtract)
                    dve.tensor_tensor(u_lo[:, k, NP:NT], t[:, NP:NT], u_hi[:, k, NP:NT].bitcast(F32),
                                      ALU.subtract).then_inc(h_ready, 1)

                scaled(0)
                for k in range(1, KT):
                    scaled(k)
                    low(k - 1)
                dve.drain()
                low(KT - 1)

            def residual(s, p, m, final=None):
                g = m_g[:, p, m, :]
                dve.tensor_tensor(sample3(xs_tmp[:]), sample3(slots[:, s, 2, LP:LP + NB * TB]), per_batch(g[:, 1:NV]), ALU.mult)
                x01 = x[:, m, 0:2 * GW].rearrange("p (g n) -> p g n", g=2)
                stt(x01, slots[:, s, 0:2, 0:GW], g[:, 0:1], x01, ALU.mult, ALU.add)
                stt(x[:, m, 2 * GW:NP], slots[:, s, 2, 0:LP], g[:, 0:1], x[:, m, 2 * GW:NP],
                    ALU.mult, ALU.add).then_inc(slot_free[s], 1)
                dve.drain()
                last = dve.tensor_tensor(x[:, m, NP:NT], x[:, m, NP:NT], xs_tmp[:], ALU.add)
                if final is not None:
                    last.then_inc(final, 1)

            def ffn(p, ada_too):
                def product():
                    dve.drain()
                    s, _, freed = jobs.take_unit()
                    dve.wait_ge(slot_free[s], freed)
                    s, done, _ = jobs.take_unit()
                    dve.wait_ge(unit_done, done)
                    dve.tensor_tensor(tile3(prod), tile3(sg), bank3(s), ALU.mult).then_inc(slot_free[s], 1)
                    prods.add()

                def low(j):
                    dve.wait_ge(hid_hi_done, prods())
                    dve.tensor_tensor(hid_lo[:, j, :], prod, hid_hi[:, j, :].bitcast(F32), ALU.subtract).then_inc(hid_ready, 1)

                def down(final=None):
                    for m in range(KT):
                        dve.drain()
                        if m % 4 < 3:
                            s, done, _ = jobs.take_part()
                            dve.wait_ge(part_done, done)
                        else:
                            s, done, _ = jobs.take_unit()
                            dve.wait_ge(unit_done, done)
                        residual(s, p, m, final)

                for j in range(2):
                    product()
                    if ada_too:
                        ada_evac("x")
                        ada_evac("y")
                    low(j)
                if ada_too:
                    dve.drain()
                    derive_gate(0)
                extra = [(batch, 1)] if ada_too else []
                with repeat(dve, FG - 1, *jobs.per(12, 6, 6), (prods, 2), *extra):
                    product()
                    down()
                    low(0)
                    product()
                    low(1)
                    if ada_too:
                        ada_evac("x")
                down(x_final)

            dve.memset(x[:, :, NT:W], 0.0)
            dve.memset(small[:], 0.0)
            dve.memset(slots[:], 0.0)
            dve.memset(mean[:], 1.0 / D)
            dve.memset(ones[:], 1.0)
            dve.memset(eps[:], EPS).then_inc(consts_ready, 1)
            dve.wait_ge(consts_in, 16 * 7)
            for n in range(4):
                ada_evac("xy"[n % 2])
            dve.drain()
            derive_norm(0, NORM1)
            dve.tensor_scalar(b_in[:, :, 0:2], b_in[:, :, 0:2], HD ** -0.5, None, ALU.mult)
            dve.tensor_scalar(b_in[:, :, 6:8], b_in[:, :, 6:8], 0.5, None, ALU.mult)
            dve.tensor_scalar(b_in[:, :, 8:12:2], b_in[:, :, 8:12:2], 0.5, None, ALU.mult)
            dve.tensor_scalar(b_in[:, :, 12:16], b_in[:, :, 12:16], 0.5, None, ALU.mult)
            dve.tensor_scalar(vecs[:, MH, :], vecs[:, MH, :], 0.5, None, ALU.mult).then_inc(biases_ready, 1)
            dve.drain()
            norm(0)
            ffn(0, True)

            dve.drain()
            dve.memset(wg_raw[:], 0.0).then_inc(wg_cleared, 1)
            derive_norm(1, NORM2)
            derive_norm(2, NORM3)
            derive_gate(1)
            derive_gate(2)
            dve.drain()
            norm(1)
            dve.drain()
            dve.wait_ge(gate_w_in, 32)
            dve.tensor_copy(wg_hi[:], wg_raw[:])
            dve.drain()
            dve.tensor_tensor(wg_lo[:], wg_raw[:], wg_hi[:].bitcast(F32), ALU.subtract).then_inc(wg_ready, 1)

            def r(i, a=0, b=NT, p=0):
                return rows[p:p + 4, i, a:b]

            dve.memset(rows[:, ROW_Q, :], 0.0)
            dve.memset(rows[0:4, ROW_1, :], 1.0)
            dve.memset(mc[:], 0.0).then_inc(rows_dve, 1)
            dve.drain()
            jobs.take_part()
            dve.wait_ge(rows_act, 1)
            stt(r(ROW_Z), r(ROW_Z), 0.0, r(ROW_E), ALU.min, ALU.subtract)
            dve.drain()
            segs = [seg("p", i) for i in range(NC)] + [seg("s", i) for i in range(NB)]
            for a, L in segs:
                dve.tensor_tensor_scan(r(ROW_B, a, a + L), r(ROW_1, a, a + L), r(ROW_Z, a, a + L), 0.0, ALU.mult, ALU.add)
            dve.drain()
            dve.tensor_tensor(r(ROW_Q), r(ROW_I), r(ROW_B), ALU.subtract)
            dve.drain()
            for i, (a, L) in enumerate(segs):
                m0 = mc[:, i:i + 1] if i < NC else ms[:, i - NC:i - NC + 1]
                dve.tensor_tensor_scan(g_row[:, a:a + L], r(ROW_Q, a, a + L), r(ROW_Q, a, a + L), m0, ALU.max, ALU.max)
                if i < NC:
                    dve.drain()
                    dve.tensor_tensor(mc[:, i + 1:i + 2], g_row[:, a + L - 1:a + L], r(ROW_B, a + L - 1, a + L), ALU.add)
                    dve.drain()
            dve.drain()
            dve.tensor_copy(m_fin[:, 0:1], mc[:, NC:NC + 1])
            dve.tensor_tensor(m_fin[:, 1:1 + NB], g_row[:, NP + TB - 1:NT:TB], r(ROW_B, NP + TB - 1, NT)[:, ::TB], ALU.add).then_inc(m_ready, 1)
            gp = g_row[:, 0:NP].rearrange("p (c l) -> p c l", c=NC)
            gs = g_row[:, NP:NT].rearrange("p (c l) -> p c l", c=NB)

            def rp(i):
                return r(i, 0, NP).rearrange("p (c l) -> p c l", c=NC)

            def rs(i):
                return r(i, NP, NT).rearrange("p (c l) -> p c l", c=NB)

            dve.tensor_tensor(rp(ROW_I), mc[:, 0:NC].unsqueeze(2).to_broadcast([4, NC, CH]), gp, ALU.subtract)
            dve.tensor_tensor(rs(ROW_I), ms[:].unsqueeze(2).to_broadcast([4, NB, TB]), gs, ALU.subtract)
            dve.tensor_tensor(r(ROW_Z), r(ROW_B), g_row[:], ALU.add).then_inc(rows_dve, 1)
            dve.tensor_tensor(rp(ROW_T), rp(ROW_Q), gp[:, :, CH - 1:CH].to_broadcast([4, NC, CH]), ALU.subtract)
            dve.tensor_tensor(rs(ROW_T), rs(ROW_Q), gs[:, :, TB - 1:TB].to_broadcast([4, NB, TB]), ALU.subtract).then_inc(rows_dve, 1)
            dve.wait_ge(rows_act, 2)
            dve.tensor_copy(apv[:, 0:NC], rows[32:36, ROW_Q, CH - 1:NP:CH])
            dve.tensor_copy(apv[:, NC:NC + NB], rows[32:36, ROW_Q, NP + TB - 1:NT:TB]).then_inc(rows_dve, 1)

            def conv_gate(t):
                s, _, freed = jobs.take_unit()
                dve.drain()
                dve.wait_ge(slot_free[s], freed)
                dve.tensor_scalar(th[:, t, :], th[:, t, :], 0.5, 0.5, ALU.mult, ALU.add)

            def conv_value(h1, t):
                dve.drain()
                s, done, _ = jobs.take_unit()
                dve.wait_ge(unit_done, done)
                if convs[t].turn is not None:
                    dve.wait_ge(conv_out[t], 16 * convs[t]())
                convs[t].add(2)
                b = bias_of(h1, 9 + 2 * t)
                stt(glu[:, t, PAST:PAST + 2 * GW].rearrange("p (g n) -> p g n", g=2), slots[:, s, 0:2, 0:GW], b,
                    th[:, t, 0:2 * GW].rearrange("p (g n) -> p g n", g=2), ALU.add, ALU.mult)
                stt(glu[:, t, PAST + 2 * GW:PAST + NP], slots[:, s, 2, 0:LP], b, th[:, t, 2 * GW:NP], ALU.add, ALU.mult)
                stt(glus[:, t, :, PAST:PAST + TB], sample3(slots[:, s, 2, LP:LP + NB * TB]), b,
                    sample3(th[:, t, NP:NT]), ALU.add, ALU.mult).then_inc(slot_free[s], 1)

            convs = [Tally(), Tally()]
            dve.memset(glu[:, :, 0:PAST], 0.0)
            conv_gate(0)
            conv_value(0, 0)
            conv_gate(1)
            conv_value(0, 1)

            for n in range(4):
                bank, full, free, use = ((bank_x, x_full, x_free, xu), (bank_y, y_full, y_free, yu))[n % 2]
                dve.wait_ge(full, use.add())
                L = P if n < 2 else TB
                dst = (col if n < 2 else cols)[:, 4 * (n % 2):4 * (n % 2) + 4, :]
                src = bank[0:L].rearrange("p (c q e) -> p c q e", c=4, q=4)[:, :, :, 0:4]
                dve.tensor_copy(dst.rearrange("p c (q h) -> p c q h", q=4), src).then_inc(free, 1)
            dve.memset(y[:, :, NT:W], 0.0)
            dve.memset(vaug[:, HD:C1], 1.0)
            dve.memset(b_cur[:, :, NT:W], 0.0).then_inc(b_out, 16)
            dve.memset(c_cur[:], 0.0).then_inc(c_out, 16)
            for n in range(3):
                dve.memset(st[:, n], 0.0).then_inc(st_out[n], 16)
            for t in range(2):
                dve.memset(th[:, t, NT:W], 0.0).then_inc(th_out[t], 16)
            dve.drain()

            def prelude(h):
                of_head = (lambda t, n: t[:, :, h:16:4]) if isinstance(h, int) else (
                    lambda t, n: t.rearrange("p c (q h) -> p c q h", q=4)[:, :, :, bass.ds(h, 1)].rearrange("p c q h -> p c (q h)"))
                sel = ident[0:4, h:h + 1] if isinstance(h, int) else ident[0:4, bass.ds(h, 1)]
                dve.drain()
                dve.wait_ge(c_out, 16 * heads(1))
                dve.wait_ge(b_out, 16 * heads(1))
                dve.tensor_copy(col_h[:], of_head(col[:], NC))
                dve.tensor_copy(cols_h[:], of_head(cols[:], NB))
                dve.tensor_scalar(g_cur[:], g_row[:], sel, -1.0, ALU.mult, ALU.mult)
                dve.tensor_scalar(apm[:], apv[:], sel, None, ALU.mult)
                dve.memset(c_cur[:], 0.0).then_inc(head_ready, 1)
                heads.add()

            def taps(h):
                tiles = [2 * h, 2 * h + 1]
                pick = lambda t: (y[:, tiles[t], :] if isinstance(h, int) else y[:, bass.ds(tiles[t], 1), :].rearrange("p a n -> p (a n)"))
                if isinstance(h, int):
                    dve.tensor_copy(dw_cur[:], w_dw[:, 2 * h:2 * h + 2, :])
                else:
                    dve.tensor_copy(dw_cur[:], w_dw[:, bass.ds(2 * h, 2), :])
                for j in range(CW):
                    dve.drain()
                    if j == 0:
                        dve.wait_ge(glus_in, 32 * heads())
                    for t in range(2):
                        yt = pick(t)
                        w = dw_cur[:, t, j:j + 1]
                        for out, src in ((yt[:, 0:NP], glu[:, t, j:j + NP]),
                                         (sample3(yt[:, NP:NT]), glus[:, t, :, j:j + TB])):
                            if j == 0:
                                b = vecs[:, B_DW, 2 * h + t:2 * h + t + 1] if isinstance(h, int) else vecs[:, B_DW, bass.ds(2 * h + t, 1)]
                                last = dve.tensor_scalar(out, src, w, b, ALU.mult, ALU.add)
                            else:
                                last = stt(out, src, w, out, ALU.mult, ALU.add)
                last.then_inc(taps_done, 1)

            def section_a(h):
                prelude(h)
                taps(h)
                for _ in range(6):
                    jobs.take_unit()
                for t in range(2):
                    s, _, freed = jobs.take_unit()
                    dve.wait_ge(slot_free[s], freed)
                    dve.tensor_scalar(qkvo[:, 6 + t, :], qkvo[:, 6 + t, :], 1.0, None, ALU.add)

            def piece(h, kind, i, stage):
                if i < 0:
                    return
                a, L = seg(kind, i)
                c = col_h[:, i, :] if kind == "p" else cols_h[:, i, :]
                mem = c_cur if kind == "p" else st[:, i % 3]
                if stage == 0:
                    xu.add()
                    dve.wait_ge(d_ready, steps.add())
                    yu.add()
                    dve.tensor_copy(vws[0:L, HD:C1], c[0:L, 3:4])
                    dve.tensor_tensor(pw[0:L, 0:L], bank_y[0:L, 0:L], dw[0:L, 0:L], ALU.mult).then_inc(y_free, 1)
                elif stage == 1:
                    dve.drain()
                    dve.wait_ge(y_full, yu.add())
                    dve.wait_ge(x_free, xu.add())
                    dve.tensor_tensor(hn[0:L, :], bank_y[0:L, 0:C1], tin[0:L, :], ALU.add).then_inc(y_free, 1)
                    dve.drain()
                    stt(small[0:L, 3:4], hn[0:L, HD:C1], -1.0, hn[0:L, HD:C1], ALU.mult, ALU.max)
                    dve.drain()
                    dve.tensor_tensor(small[0:L, 3:4], small[0:L, 3:4], c[0:L, 2:3], ALU.max)
                    dve.drain()
                    dve.reciprocal(small[0:L, 0:1], small[0:L, 3:4]).then_inc(rd_ready, 1)
                elif stage == 2:
                    ap = ap_h[:, i:i + 1] if kind == "p" else ap_h[:, NC + i:NC + i + 1]
                    for m, (bank, full, free, use) in enumerate(((bank_x, x_full, x_free, xu), (bank_y, y_full, y_free, yu))):
                        dve.wait_ge(full, use.add())
                        stt(mem[:, m, :], mem[:, m, :], ap, bank[:, 0:C1], ALU.mult, ALU.add).then_inc(free, 1)
                    dve.wait_ge(r_ready, steps())
                    dve.reciprocal(small[0:L, 4:5], small[0:L, 2:3])
                    dve.drain()
                    dve.tensor_scalar(hs_of[kind][0:L, :], hn[0:L, 0:HD], small[0:L, 0:1], small[0:L, 4:5],
                                      ALU.mult, ALU.mult).then_inc(hs_ready, 1)
                else:
                    dve.wait_ge(x_full, xu.add())
                    for m in range(2):
                        g = vecs[:, MH, 2 * h + m:2 * h + m + 1] if isinstance(h, int) else vecs[:, MH, bass.ds(2 * h + m, 1)]
                        last = stt(b_cur[:, m, a:a + L], bank_x[:, m * P:m * P + L], g, qkvo[:, 6 + m, a:a + L], ALU.mult, ALU.mult)
                    last.then_inc(x_free, 1)
                    dve.drain()

            def section_b(h, n_units):
                dve.drain()
                dve.wait_ge(x_full, xu.add())
                dve.tensor_copy(ap_h[:], bank_x[:, 0:NC + NB]).then_inc(x_free, 1)
                dve.drain()
                each = len(PIECES) // (KT * n_units)
                for n in range(n_units):
                    for q in PIECES[n * KT * each:(n + 1) * KT * each]:
                        piece(h, *q)
                    if n_units == 8 and n < 4:
                        if n % 2 == 0:
                            conv_gate(n // 2)
                        else:
                            conv_value(h + 1, n // 2)
                    else:
                        jobs.take_unit()
                piece(h, "s", NB - 1, 3)

            with repeat(dve, H - 1, *jobs.per(16, 16, 0), (xu, 65), (yu, 48), (steps, 16), (heads, 1), (convs[0], 2), (convs[1], 2)) as h:
                section_a(h)
                section_b(h, 8)
            section_a(H - 1)
            section_b(H - 1, 4)

            for k in range(KT):
                dve.wait_ge(b_hi_done, k + 1)
                dve.tensor_tensor(u_lo[:, k, :], b_cur[:, k % 2, :], u_hi[:, k, :].bitcast(F32), ALU.subtract).then_inc(b_ready, 1)
            ysum, yss = a_tmp[:, 5], b_cur[:, 0]
            dve.drain()
            for k in range(1, KT):
                last = dve.tensor_tensor(ysum, y[:, 0, :] if k == 1 else ysum, y[:, k, :], ALU.add)
                if k == KT - 1:
                    last.then_inc(y_cent, 1)
                dve.drain()

            for n in range(3):
                dve.wait_ge(st_out[n], 16 * [13, 13, 9][n])
            dve.wait_ge(c_out, 16 * (H + 1))
            for t in range(2):
                dve.wait_ge(conv_out[t], 16 * KT)

            def gated(n):
                m = n % KT
                s, done, _ = jobs.take_unit()
                dve.wait_ge(unit_done, done)
                dve.wait_ge(g_back[n % 2], 16 * (n // 2 + 1))
                if n < KT:
                    stt(tile3(z[:, m, :]), tile3(th[:, n % 2, :]), 1.0, bank3(s), ALU.add, ALU.mult).then_inc(slot_free[s], 1)
                else:
                    dve.drain()
                    stt(tile3(th[:, n % 2, :]), tile3(th[:, n % 2, :]), 1.0, bank3(s), ALU.add, ALU.mult).then_inc(slot_free[s], 1)
                    dve.drain()
                    dve.tensor_tensor(z[:, m, :], z[:, m, :], th[:, n % 2, :], ALU.add).then_inc(z_done, 1)

            gated(0)
            gated(1)
            s, done, _ = jobs.take_part()
            dve.wait_ge(part_done, done)
            dve.tensor_copy(tile3(ysum), bank3(s)).then_inc(slot_free[s], 1)
            dve.drain()
            for k in range(KT):
                dve.tensor_tensor(y[:, k, :], y[:, k, :], ysum, ALU.subtract).then_inc(y_cent, 1)
                if k:
                    dve.drain()
                    dve.wait_ge(ysq_done, k)
                    if k == 1:
                        dve.tensor_copy(yss[:, 0:NT], a_tmp[:, 6, 0:NT]).then_inc(ysq_added, 1)
                    else:
                        dve.tensor_tensor(yss[:, 0:NT], yss[:, 0:NT], a_tmp[:, 6 + (k - 1) % 2, 0:NT], ALU.add).then_inc(ysq_added, 1)
                if k == 4:
                    gated(2)
            dve.drain()
            dve.wait_ge(ysq_done, KT)
            dve.tensor_tensor(yss[:, 0:NT], yss[:, 0:NT], a_tmp[:, 7, 0:NT], ALU.add).then_inc(ysq_added, 1)
            gated(3)
            gated(4)
            s, _, freed = jobs.take_part()
            dve.drain()
            dve.wait_ge(slot_free[s], freed)
            dve.reciprocal(yss, yss)
            dve.drain()

            def a_low(k):
                dve.wait_ge(a_hi_done, k + 1)
                dve.tensor_tensor(a_lo[:, k, :], y[:, k, :], a_hi[:, k, :].bitcast(F32), ALU.subtract).then_inc(a_ready, 1)

            for k in range(KT):
                dve.tensor_tensor(y[:, k, :], y[:, k, :], yss, ALU.mult).then_inc(y_norm, 1)
                if k:
                    a_low(k - 1)
                if k in (2, 5):
                    gated(5 + k // 3)
            a_low(KT - 1)
            gated(7)
            for n in range(KT, 2 * KT):
                gated(n)
                dve.wait_ge(z_hi_done, n - KT + 1)
                dve.tensor_tensor(u_lo[:, n - KT, :], z[:, n - KT, :], u_hi[:, n - KT, :].bitcast(F32), ALU.subtract).then_inc(z_ready, 1)
            for m in range(KT):
                dve.drain()
                s, done, _ = jobs.take_unit()
                dve.wait_ge(unit_done, done)
                dve.wait_ge(x_back[m], 16)
                residual(s, 1, m, x_final)
            norm(2)
            ffn(2, False)
            sum_squares(3)
            for k in range(KT):
                dve.drain()
                if k >= 4:
                    dve.wait_ge(out_done[k % 4], 16 * (k // 4))
                stt(work[:, 4 + k % 4, 0:NT], x[:, k, 0:NT], vecs[:, NORMF, k:k + 1], rstd[:, 0:NT],
                    ALU.mult, ALU.mult).then_inc(out_ready, 1)


def _tiles(w):
    n = w.shape[1] // P
    return w.reshape(KT, P, n, P).transpose(2, 1, 0, 3).reshape(n, P, D)


def _down(w):
    return w.reshape(FG, 2, P, 2, 512).transpose(0, 3, 2, 1, 4).reshape(FG, 2, P, D)


def _ffn_units(gate, up, down):
    g, u, d = _tiles(gate), _tiles(up), _down(down)
    out = [g[0], u[0], g[1], u[1]]
    for i in range(1, FG):
        out += [g[2 * i], u[2 * i], d[i - 1][0], d[i - 1][1], g[2 * i + 1], u[2 * i + 1]]
    return out + [d[FG - 1][0], d[FG - 1][1]]


def _mixer_units(w_in):
    cv, cg, q, k, v, o, ga, gb = (_tiles(w_in[:, i * D:(i + 1) * D]) for i in range(8))
    out = [cg[0], cv[0], cg[1], cv[1]]
    for h in range(H):
        a, b = 2 * h, 2 * h + 1
        out += [q[a], q[b], k[a], k[b], v[a], v[b], o[a], o[b]]
        if h < H - 1:
            out += [cg[a + 2], cv[a + 2], cg[b + 2], cv[b + 2]]
        out += [ga[a], ga[b], gb[a], gb[b]]
    return out


def kernel(**inputs):
    import concourse.bacc as bacc
    from concourse.bass_utils import run_bass_kernel_spmd

    a = {k: np.asarray(v) for k, v in inputs.items()}
    w_in = a["w_in"][0]
    units = (_ffn_units(a["w1_gate"][0], a["w1_up"][0], a["w1_down"][0]) + _mixer_units(w_in)
             + list(_tiles(a["w_mlstm_out"][0])) + list(_tiles(a["w_conv_out"][0])) + list(_tiles(a["w_out"][0]))
             + _ffn_units(a["w2_gate"][0], a["w2_up"][0], a["w2_down"][0]))
    cv, cg, q, k, v, o, ga, gb = a["b_in"][0, :8 * D].reshape(8, H, 2, P)
    b_in = np.stack([q[:, 0], q[:, 1], k[:, 0], k[:, 1], v[:, 0], v[:, 1], o[:, 0], o[:, 1],
                     cg[:, 0], cv[:, 0], cg[:, 1], cv[:, 1], ga[:, 0], ga[:, 1], gb[:, 0], gb[:, 1]], 1)
    vecs = np.stack([a["norm_ffn1"][0], a["norm_mix"][0], a["norm_ffn2"][0], a["final_norm"], a["b_dw"][0],
                     a["ln_conv_g"][0], a["ln_conv_b"][0], a["mh_norm"][0].reshape(D)])
    state = np.concatenate([a["state_C"][0].transpose(1, 0, 3, 2).reshape(H, NB, 2, P, HD),
                            a["state_n"][0].transpose(1, 0, 2).reshape(H, NB, 2, P, 1)], -1)
    feats = {
        "w_units": np.stack(units),
        "ada_units": _tiles(a["w_ada"][0]),
        "x_prompt": a["x_prompt"][0].reshape(NP, KT, P).transpose(2, 1, 0),
        "x_sample": a["x_sample"].reshape(NB * TB, KT, P).transpose(2, 1, 0),
        "c": np.concatenate([a["c_prompt"], a["c_sample"]]).reshape(NV, KT, P).transpose(2, 1, 0),
        "b_ada": a["b_ada"][0].reshape(NMOD * KT, P).T,
        "b_in": b_in.transpose(2, 0, 1),
        "vecs": vecs.reshape(8, KT, P).transpose(2, 0, 1),
        "w_dw": a["w_dw"][0].reshape(CW, KT, P).transpose(2, 1, 0),
        "w_if": w_in[:, 8 * D:].reshape(KT, P, 2 * H).transpose(1, 0, 2),
        "b_i": a["b_in"][0, 8 * D:8 * D + H].reshape(H, 1),
        "b_f": a["b_in"][0, 8 * D + H:].reshape(H, 1),
        "state_m": a["state_m"][0].T,
        "state_conv": a["state_conv"][0].reshape(NB, PAST, KT, P).transpose(2, 3, 0, 1),
        "state": state.transpose(0, 1, 3, 2, 4),
    }
    outs = {"y": (KT, P, NT), "conv_p": (KT, P, PAST), "conv_s": (KT, P, NB, PAST), "m": (H, 1 + NB),
            "C_p": (H, P, 2, C1), "C_s": (H, NB, P, 2, C1)}
    nc = bacc.Bacc("TRN2", target_bir_lowering=False, num_devices=1, dynamic_dma_scratch_size=64)
    arrays = {n: np.ascontiguousarray(v) for n, v in feats.items()}
    t_in = {n: nc.dram_tensor(n + "_dram", v.shape, F32, kind="ExternalInput").ap() for n, v in arrays.items()}
    t_out = {n: nc.dram_tensor(n + "_out", s, F32, kind="ExternalOutput").ap() for n, s in outs.items()}
    trunk(nc, t_in, t_out)
    res = run_bass_kernel_spmd(nc, [{n + "_dram": v for n, v in arrays.items()}], core_ids=[0]).results[0]
    r = {n: np.asarray(res[n + "_out"]) for n in outs}
    y = r["y"].reshape(D, NT).T
    c_p = r["C_p"].transpose(0, 2, 1, 3).reshape(1, 1, H, HD, C1)
    c_s = r["C_s"].transpose(1, 0, 3, 2, 4).reshape(1, NB, H, HD, C1)
    c = np.ascontiguousarray
    return (c(y[:NP]).reshape(1, NP, D), c(y[NP:]).reshape(NB, TB, D),
            c(r["conv_p"].reshape(D, PAST).T).reshape(1, 1, PAST, D),
            c(c_p[..., :HD].swapaxes(-1, -2)), c(c_p[..., HD]), c(r["m"][:, 0]).reshape(1, 1, H),
            c(r["conv_s"].reshape(D, NB, PAST).transpose(1, 2, 0)).reshape(1, NB, PAST, D),
            c(c_s[..., :HD].swapaxes(-1, -2)), c(c_s[..., HD]), c(r["m"][:, 1:].T).reshape(1, NB, H))
```

```python
from contextlib import ExitStack, contextmanager

import numpy as np
import concourse.bass as bass
from concourse import mybir
from concourse.alu_op_type import AluOpType as ALU

ACT = mybir.ActivationFunctionType
F32 = mybir.dt.float32
F32R = mybir.dt.float32r
I32 = mybir.dt.int32

P = 128
D = 1024
KT = D // P
NP = 1024
NB, TB = 8, 8
NT = NP + NB * TB
GW = 364
GROUPS = [(0, GW), (GW, 2 * GW), (2 * GW, NT)]
W = 3 * GW
LP = NP - 2 * GW
FF = 2816
FT = FF // P
FG = FT // 2
NV = 9
CW = 31
PAST = CW - 1
H = 4
HD = D // H
CH = 128
NC = NP // CH
C1 = HD + 1
NMOD = 9
EPS = 1e-6
MASKED = -1e30
ROOT_BITS = float(0x5F3759DF - 0x400000 - 2 ** 31)
AB = 4
LEAD = 4
DOWN_UNITS = (2, 3)
JOBS_FFN = 2 * FT + 8 * FG
JOBS_BEFORE_MIXER = 1 + JOBS_FFN + 1 + 1
JOBS_BEFORE_TAIL = 1 + JOBS_FFN + 1 + 1 + 8 * KT
MEANS_AFTER = (1, 4)
N_UNITS = 2 * (2 * FT + 2 * FG) + 8 * KT + 3 * KT


class Tally:

    def __init__(self, n=0):
        self.n, self.turn, self.per = n, None, 0

    def __call__(self, more=0):
        n = self.n + more
        return n if self.turn is None else self.turn * self.per + n

    def add(self, k=1):
        self.n += k
        return self()


@contextmanager
def repeat(eng, times, *tallies):
    start = [t.n for t, _ in tallies]
    with eng.Fori(0, times) as turn:
        for t, per in tallies:
            t.turn, t.per = turn, per
        yield turn
        for (t, per), n in zip(tallies, start):
            assert t.n - n == per, (t.n - n, per)
    for (t, per), n in zip(tallies, start):
        t.turn, t.n = None, n + per * times


class Jobs:

    def __init__(self):
        self.job, self.unit, self.part = Tally(), Tally(), Tally()

    def slot(self):
        return self.job.n % 2

    def used(self, more=0):
        t = self.job
        n = (t.n + more) // 2
        return n if t.turn is None else t.turn * (t.per // 2) + n

    def _take(self, tally):
        tally.add()
        s, freed = self.slot(), self.used()
        self.job.add()
        return s, tally(), freed + 1

    def take_unit(self):
        return self._take(self.unit)

    def take_part(self):
        return self._take(self.part)

    def per(self, jobs, units, parts):
        return (self.job, jobs), (self.unit, units), (self.part, parts)


def trunk(nc, t_in, t_out):
    with ExitStack() as ctx:
        at = [(nc.sbuf_base + 63) // 64 * 64]

        def region(nbytes):
            start = at[0]
            at[0] += (nbytes + 31) // 32 * 32
            assert at[0] <= nc.sbuf_usable_end, (at[0], nc.sbuf_usable_end)
            return start

        def place(name, shape, dt, offset):
            return nc.alloc_sbuf_tensor_at(name, shape, dt, offset=offset)

        def own(name, shape, dt=F32):
            return place(name, shape, dt, region(int(np.prod(shape[1:])) * 4))

        TILE = W * 4
        w_raw = own("w_raw", [P, 2, D])
        w_hi = own("w_hi", [P, 2, D], F32R)
        w_lo = own("w_lo", [P, 2, D], F32R)
        u_hi = own("u_hi", [P, KT, W], F32R)
        u_lo = own("u_lo", [P, KT, W], F32R)
        r_x = region(KT * TILE)
        x = place("x", [P, KT, W], F32, r_x)
        qkvo = place("qkvo", [P, 8, W], F32, r_x)
        a_hi = place("a_hi", [P, KT, W], F32R, r_x)
        a_tmp = place("a_tmp", [P, KT, W], F32, r_x)
        r_y = region(KT * TILE)
        y = place("y", [P, KT, W], F32, r_y)
        a_lo = place("a_lo", [P, KT, W], F32R, r_y)
        work = place("work", [P, KT, W], F32, r_y)
        sg, prod, ss, rstd = (work[:, i] for i in (0, 1, 2, 3))
        sq = [work[:, 4], work[:, 5]]
        tn = [work[:, 6], work[:, 7]]
        r_s = region(4 * TILE)
        ada = place("ada", [P, AB, D], F32, r_s)
        b_cur = place("b_cur", [P, 2, W], F32, r_s)
        th = place("th", [P, 2, W], F32, r_s + 2 * TILE)
        r_z = at[0]
        glu = own("glu", [P, 2, PAST + NP])
        glus = own("glus", [P, 2, NB, PAST + TB])
        st = own("st", [P, 3, 2, C1])
        c_cur = own("c_cur", [P, 2, C1])
        ktok = own("ktok", [P, HD])
        vaug = own("vaug", [P, C1])
        vws = own("vws", [P, C1])
        dw = own("dw", [P, P])
        tin = own("tin", [P, C1])
        hn_of = {kind: own(f"hn_{kind}", [P, C1]) for kind in "ps"}
        hs_of = {kind: own(f"hs_{kind}", [P, HD]) for kind in "ps"}
        g_row = own("g_row", [4, NT])
        g_cur = own("g_cur", [4, NT])
        if at[0] < r_z + KT * TILE:
            region(r_z + KT * TILE - at[0])
        z = place("z", [P, KT, W], F32, r_z)
        b_first = place("b_first", [P, 2, W], F32, r_z)
        hid_hi = place("hid_hi", [P, 2, W], F32R, r_z)
        hid_lo = place("hid_lo", [P, 2, W], F32R, r_z + 2 * TILE)
        mods = own("mods", [P, NMOD * KT, NV])
        m_a = own("m_a", [P, 3, KT, NV])
        m_g = own("m_g", [P, 3, KT, NV])
        r_tmp = region(NB * TB * 4)
        xs_tmp = place("xs_tmp", [P, NB * TB], F32, r_tmp)
        dw_cur = place("dw_cur", [P, 2, CW], F32, r_tmp)
        b_ada = own("b_ada", [P, NMOD * KT])
        b_in = own("b_in", [P, H, 16])
        vecs = own("vecs", [P, 8, KT])
        w_dw = own("w_dw", [P, KT, CW])
        cs = own("cs", [P, KT, NV])
        col = own("col", [P, NC, 16])
        cols = own("cols", [TB, NB, 16])
        col_h = own("col_h", [P, NC, 4])
        cols_h = own("cols_h", [TB, NB, 4])
        ap_h = own("ap_h", [P, NC + NB])
        apv = own("apv", [4, NC + NB])
        apm = own("apm", [4, NC + NB])
        small = own("small", [P, 6, 2])
        inv_den, sq_sum, half_ms, inv_rms, tmp_rms, den = (small[:, n, :] for n in range(6))
        ident = own("ident", [P, P])
        mask = own("mask", [P, P])
        mean = own("mean", [P, P])
        ones = own("ones", [4, P])
        eps = own("eps", [P, 1])
        one = own("one", [P, 1])
        b_if = own("b_if", [P, 1])
        mc = own("mc", [4, NC + 1])
        ms = own("ms", [4, NB])
        m_fin = own("m_fin", [4, 1 + NB])
        wg_hi = place("wg_hi", [P, KT, 36], F32R, r_z)
        wg_lo = place("wg_lo", [P, KT, 36], F32R, r_z + KT * 36 * 4)
        wg_raw = place("wg_raw", [P, KT, 36], F32, r_z + 2 * KT * 36 * 4)
        rows = place("rows", [P, KT, W], F32, r_y)
        NORM1, NORM2, NORM3, NORMF, B_DW, LN_G, LN_B, MH = range(8)
        ROW_I, ROW_Z, ROW_E, ROW_1, ROW_B, ROW_T, ROW_Q = range(7)

        slots = ctx.enter_context(nc.psum_tensor("slots", [P, 2, 3, 512], F32))
        bank_x = ctx.enter_context(nc.psum_tensor("bank_x", [P, 512], F32))
        bank_y = ctx.enter_context(nc.psum_tensor("bank_y", [P, 512], F32))

        x_keep = nc.dram_tensor("x_keep", (P, KT, W), F32, kind="Internal").ap()
        b_keep = nc.dram_tensor("b_keep", (H, P, 2, W), F32, kind="Internal").ap()
        ga_keep = nc.dram_tensor("ga_keep", (KT, P, W), F32, kind="Internal").ap()
        gb_keep = nc.dram_tensor("gb_keep", (KT, P, W), F32, kind="Internal").ap()

        def sem(name):
            return ctx.enter_context(nc.semaphore(name))

        x_in, c_in, consts_in, gate_w_in = (sem(n) for n in ("x_in", "c_in", "consts_in", "gate_w_in"))
        w_in = [sem(f"w_in{i}") for i in range(2)]
        ada_in = [sem(f"ada_in{i}") for i in range(AB)]
        w_split, unit_done, part_done = sem("w_split"), sem("unit_done"), sem("part_done")
        w_hi_done = sem("w_hi_done")
        slot_free = [sem("slot_free0"), sem("slot_free1")]
        tables = sem("tables")
        consts_ready, biases_ready, wg_cleared = (sem(n) for n in ("consts_ready", "biases_ready", "wg_cleared"))
        cs_ready, ada_used, ada_free = sem("cs_ready"), sem("ada_used"), sem("ada_free")
        sq_done, sq_added, t_ready, hi_ready, h_ready = (sem(n) for n in ("sq_done", "sq_added", "t_ready", "hi_ready", "h_ready"))
        x_final = sem("x_final")
        hid_hi_done, hid_ready = sem("hid_hi_done"), sem("hid_ready")
        x_out, x_tile = sem("x_out"), [sem(f"x_tile{k}") for k in range(KT)]
        wg_ready, rows_act, rows_dve = sem("wg_ready"), sem("rows_act"), sem("rows_dve")
        x_full, x_free, y_full, y_free = sem("x_full"), sem("x_free"), sem("y_full"), sem("y_free")
        o_ready = sem("o_ready")
        head_ready, d_ready, rd_ready, r_ready, hs_ready = (sem(n) for n in ("head_ready", "d_ready", "rd_ready", "r_ready", "hs_ready"))
        st_in, st_out = [sem(f"st_in{i}") for i in range(3)], [sem(f"st_out{i}") for i in range(3)]
        c_out, m_out, b_out = sem("c_out"), sem("m_out"), sem("b_out")
        m_ready = sem("m_ready")
        th_out = [sem("th_out0"), sem("th_out1")]
        taps_done, glus_in, conv_out = sem("taps_done"), sem("glus_in"), [sem("conv_out0"), sem("conv_out1")]
        b_back = [sem(f"b_back{k}") for k in range(6)]
        g_back = [sem("g_back0"), sem("g_back1")]
        b_hi_done, b_ready = sem("b_hi_done"), sem("b_ready")
        y_cent, ysq_done, ysq_added, y_norm, a_hi_done, a_ready = (
            sem(n) for n in ("y_cent", "ysq_done", "ysq_added", "y_norm", "a_hi_done", "a_ready"))
        z_done, z_hi_done, z_ready = sem("z_done"), sem("z_hi_done"), sem("z_ready")
        out_ready, out_done = sem("out_ready"), [sem(f"out_done{i}") for i in range(4)]

        b_tiles = [b_first[:, k, :] for k in range(2)] + [qkvo[:, k, :] for k in range(4)] + [b_cur[:, k, :] for k in range(2)]

        def bank3(s):
            return slots[:, s, :, 0:GW]

        def tile3(ap):
            return ap.rearrange("p (g n) -> p g n", g=3)

        def per_batch(ap8):
            return ap8.unsqueeze(2).to_broadcast([P, NB, TB])

        def sample3(ap64):
            return ap64.rearrange("p (b t) -> p b t", b=NB)

        def pieces():
            out = []
            for i in range(NC):
                out += [("p", i, 0), ("p", i - 1, 3), ("p", i, 1), ("p", i, 2),
                        ("s", i, 0), ("s", i - 1, 3), ("s", i, 1), ("s", i, 2)]
            return out
        PIECES = pieces()

        def pieces_at(n_units, n, k=None):
            lead = LEAD * n_units // 8
            upto = lambda tiles: max(tiles - lead, 0) * len(PIECES) // (n_units * KT - lead)
            first, last = (n * KT, (n + 1) * KT) if k is None else (n * KT + k, n * KT + k + 1)
            return PIECES[upto(first):upto(last)]

        def seg(kind, i):
            return (i * CH, CH) if kind == "p" else (NP + i * TB, TB)

        def bias_of(h, j):
            return b_in[:, h, j:j + 1] if isinstance(h, int) else b_in[:, bass.ds(h, 1), j:j + 1].rearrange("p a b -> p (a b)")

        def at_tile(t, n, merge):
            return t[n] if isinstance(n, int) else t[bass.ds(n, 1)].rearrange(merge)

        block = ctx.enter_context(nc.Block())

        @block.sync
        def _(sp):
            unit, batch = Tally(), Tally()

            def load_unit():
                slot = unit.n % 2
                if unit.n >= 2:
                    sp.wait_ge(w_split, unit(-1))
                n = unit()
                src = t_in["w_units"][n] if unit.turn is None else t_in["w_units"][bass.ds(n, 1)].rearrange("o p n -> p (o n)")
                sp.dma_start(w_raw[:, slot, :], src).then_inc(w_in[slot], 16)
                unit.add()

            def load_ada_tile(j):
                if batch.n >= 1:
                    sp.wait_ge(ada_used, (batch() - 1) * AB + j + 1)
                n = batch() * AB + j
                src = t_in["ada_units"][n] if batch.turn is None else t_in["ada_units"][bass.ds(n, 1)].rearrange("o p n -> p (o n)")
                sp.dma_start(ada[:, j, :], src).then_inc(ada_in[j], 16)
                if j == AB - 1:
                    batch.add()

            def load_ada():
                for j in range(AB):
                    load_ada_tile(j)

            sp.dma_start(cs[:], t_in["c"]).then_inc(c_in, 16)
            load_ada()
            for dst, name in ((b_ada, "b_ada"), (b_in, "b_in"), (vecs, "vecs"), (w_dw, "w_dw")):
                sp.dma_start(dst[:], t_in[name]).then_inc(consts_in, 16)
            sp.dma_start(b_if[0:4, :], t_in["b_i"]).then_inc(consts_in, 16)
            sp.dma_start(b_if[32:36, :], t_in["b_f"]).then_inc(consts_in, 16)
            sp.dma_start(ms[:], t_in["state_m"]).then_inc(consts_in, 16)
            sp.dma_start(x[:, :, NP:NT], t_in["x_sample"]).then_inc(x_in, 16)
            for k in range(KT):
                sp.dma_start(x[:, k, 0:NP], t_in["x_prompt"][:, k, :]).then_inc(x_tile[k], 16)
                load_ada_tile(k % AB)
            load_ada()
            load_unit()
            load_unit()
            load_unit()
            for _ in range(4):
                load_ada()
                if unit.n < 4:
                    load_unit()
            with repeat(sp, FG - 1, (unit, 6), (batch, 1)):
                for n in range(6):
                    load_unit()
                    if n not in DOWN_UNITS:
                        load_ada_tile(n if n < 2 else n - 2)
            load_unit()
            load_unit()
            load_unit()
            load_unit()
            sp.wait_ge(wg_cleared, 1)
            sp.dma_start(wg_raw[:, :, 0:4], t_in["w_if"][:, :, 0:4]).then_inc(gate_w_in, 16)
            sp.dma_start(wg_raw[:, :, 32:36], t_in["w_if"][:, :, 4:8]).then_inc(gate_w_in, 16)
            sp.wait_ge(x_final, KT)
            sp.dma_start(x_keep, x[:]).then_inc(x_out, 16)
            for t in range(2):
                sp.dma_start(glus[:, t, :, 0:PAST], t_in["state_conv"][t]).then_inc(glus_in, 16)
            jobs = Jobs()
            jobs.job.n = JOBS_BEFORE_MIXER
            xu, yu, heads = Tally(2), Tally(2), Tally()
            stores = [Tally(1) for _ in range(3)]

            def st_dram(t, h, b):
                return t[h, b] if isinstance(h, int) else t[bass.ds(h, 1), b].rearrange("o p m c -> p (o m) c")

            def load_state(h, b):
                sp.wait_ge(st_out[b % 3], 16 * stores[b % 3]())
                sp.dma_start(st[:, b % 3], st_dram(t_in["state"], h, b)).then_inc(st_in[b % 3], 16)

            def head(h, n_units):
                for _ in range(4):
                    load_unit()
                load_state(h, 0)
                load_state(h, 1)
                for _ in range(4):
                    load_unit()
                for _ in range(8):
                    jobs.take_unit()
                for n in range(n_units):
                    for kind, i, stage in pieces_at(n_units, n):
                        if stage == 3:
                            continue
                        yu.add()
                        if kind == "s" and stage == 2:
                            sp.wait_ge(y_free, yu())
                            sp.dma_start(st_dram(t_out["C_s"], h, i), st[:, i % 3]).then_inc(st_out[i % 3], 16)
                            stores[i % 3].add()
                            if i + 2 < NB:
                                load_state(h, i + 2)
                    if n_units == 4 and n == 3:
                        for k in range(2, 6):
                            sp.dma_start(qkvo[:, k - 2, :], b_keep[k // 2, :, k % 2, :]).then_inc(b_back[k], 16)
                    load_unit()
                    s, _, freed = jobs.take_unit()
                    t = n // 2 if n_units == 8 and n < 4 else n % 2
                    if n_units == 4 and n == 0:
                        sp.wait_ge(taps_done, H)
                        sp.wait_ge(b_out, 16 * H)
                        for k in range(2):
                            sp.dma_start(b_first[:, k, :], b_keep[0, :, k, :]).then_inc(b_back[k], 16)
                    if n_units == 8 and n == 0:
                        sp.wait_ge(taps_done, heads(1))
                        for c in range(2):
                            sp.dma_start(glus[:, c, :, 0:PAST],
                                         t_in["state_conv"][bass.ds(2 * h + 2 + c, 1)].rearrange("o p b n -> p (o b) n")
                                         ).then_inc(glus_in, 16)
                    if n_units == 8 and n < 4:
                        if n % 2:
                            arrived = 32 * heads(2)
                            sp.wait_ge(slot_free[s], freed)
                            sp.wait_ge(glus_in, arrived)
                            conv_stores(h + 1, t)
                    else:
                        j = n - (n_units - 4)
                        sp.wait_ge(slot_free[s], freed)
                        dst = at_tile(ga_keep if j < 2 else gb_keep, 2 * h + t, "o p n -> p (o n)")
                        sp.dma_start(dst, th[:, t, :]).then_inc(th_out[t], 16)
                heads.add()
                sp.wait_ge(x_free, xu.add(65))
                if n_units == 8:
                    sp.dma_start(at_tile(b_keep, h, "o p m n -> p (o m) n"), b_cur[:]).then_inc(b_out, 16)
                sp.dma_start(at_tile(t_out["C_p"], h, "o p m n -> p (o m) n"), c_cur[:]).then_inc(c_out, 16)

            def conv_stores(h1, t):
                sp.dma_start(at_tile(t_out["conv_p"], 2 * h1 + t, "o p n -> p (o n)"),
                             glu[:, t, NP:NP + PAST]).then_inc(conv_out[t], 16)
                sp.dma_start(at_tile(t_out["conv_s"], 2 * h1 + t, "o p b n -> p (o b) n"),
                             glus[:, t, :, TB:TB + PAST]).then_inc(conv_out[t], 16)

            load_unit()
            load_unit()
            for t in range(2):
                load_unit()
                load_unit()
                jobs.take_unit()
                s, _, freed = jobs.take_unit()
                sp.wait_ge(slot_free[s], freed)
                sp.wait_ge(glus_in, 32)
                conv_stores(0, t)
            sx = [(stores[0], 3), (stores[1], 3), (stores[2], 2)]
            with repeat(sp, H - 1, (unit, 16), (xu, 65), (yu, 48), (heads, 1), *jobs.per(16, 16, 0), *sx) as h:
                head(h, 8)
            head(H - 1, 4)
            tail = Jobs()
            tail.job.n = JOBS_BEFORE_TAIL
            reads = []
            for m in range(KT):
                reads.append(tail.take_unit()[::2])
                if m in MEANS_AFTER:
                    tail.take_part()

            def load_gate(n):
                src = (gb_keep if n < KT else ga_keep)[n % KT]
                if n >= 2:
                    if n - 2 < KT:
                        sp.wait_ge(slot_free[reads[n - 2][0]], reads[n - 2][1])
                    else:
                        sp.wait_ge(z_done, n - 1 - KT)
                sp.dma_start(th[:, n % 2, :], src).then_inc(g_back[n % 2], 16)

            for s in range(2):
                sp.wait_ge(th_out[s], 16 * (KT + 1))
            load_gate(0)
            load_gate(1)
            for n in range(2 * KT - 2):
                load_unit()
                load_gate(n + 2)
            sp.wait_ge(unit_done, unit.n - 2)
            for k in range(KT):
                sp.dma_start(x[:, k, :], x_keep[:, k, :]).then_inc(x_tile[k], 16)
            for _ in range(KT - 2):
                load_unit()
            for _ in range(4):
                load_unit()
            with repeat(sp, FG - 1, (unit, 6)):
                for _ in range(6):
                    load_unit()
            load_unit()
            load_unit()
            assert unit.n == N_UNITS, (unit.n, N_UNITS)
            for k in range(KT):
                sp.wait_ge(out_ready, k + 1)
                sp.dma_start(t_out["y"][k], work[:, 4 + k % 4, 0:NT]).then_inc(out_done[k % 4], 16)
            for n in range(4):
                sp.wait_ge(out_done[n], 16 * KT // 4)
            for t in range(2):
                sp.wait_ge(conv_out[t], 16 * KT)
            sp.wait_ge(m_out, 16)
            for n in range(3):
                sp.wait_ge(st_out[n], 16 * stores[n]())
            sp.wait_ge(c_out, 16 * (H + 1))

        @block.gpsimd
        def _(pool):
            unit = Tally()
            pool.memset(ident[:], 0.0).then_inc(tables, 1)
            pool.memset(mask[:], 0.0).then_inc(tables, 1)
            pool.memset(one[:], 1.0).then_inc(tables, 1)
            pool.wait_ge(tables, 3)
            pool.affine_select(out=ident[:], in_=ident[:], compare_op=ALU.not_equal, fill=1.0, base=0,
                               pattern=[[-1, P]], channel_multiplier=1).then_inc(tables, 1)
            pool.affine_select(out=mask[:], in_=mask[:], compare_op=ALU.is_ge, fill=MASKED, base=0,
                               pattern=[[1, P]], channel_multiplier=-1).then_inc(tables, 1)

            def split(slot, first):
                pool.wait_ge(w_in[slot], (unit() - slot) * 8 + 16)
                if not first:
                    pool.wait_ge(unit_done, unit(-1))
                pool.tensor_tensor(w_hi[:, slot, :], w_raw[:, slot, :], one[:].to_broadcast([P, D]), ALU.mult).then_inc(w_hi_done, 1)
                pool.wait_ge(w_hi_done, unit(1))
                pool.tensor_tensor(w_lo[:, slot, :], w_raw[:, slot, :], w_hi[:, slot, :].bitcast(F32),
                                   ALU.subtract).then_inc(w_split, 1)
                unit.add()

            split(0, True)
            split(1, True)
            with repeat(pool, N_UNITS // 2 - 1, (unit, 2)):
                split(0, False)
                split(1, False)

        @block.tensor
        def _(pe):
            jobs, batch = Jobs(), Tally()
            hid = Tally()
            xu, yu = Tally(), Tally()
            steps, heads = Tally(), Tally()
            sts = [Tally() for _ in range(3)]

            def open_slot():
                s = jobs.slot()
                if jobs.job.n >= 2:
                    pe.wait_ge(slot_free[s], jobs.used())
                return s

            def three_passes(s, w_of, hi, lo, k, K, middle=None):
                for q, (w, r) in enumerate(((w_hi, hi), (w_hi, lo), (w_lo, hi))):
                    if middle and q == 2:
                        middle(k)
                    for g, (a, b) in enumerate(GROUPS):
                        last = pe.matmul(slots[:, s, g, 0:b - a], w_of(w), r[:, k, a:b],
                                         start=(k == 0 and q == 0), stop=(k == K - 1 and q == 2))
                return last

            def project(hi, lo, ready=None, base=0, between=None, middle=None):
                s = open_slot()
                u = jobs.unit.n % 2
                pe.wait_ge(w_split, jobs.unit(1))
                for k in range(KT):
                    if ready is not None:
                        pe.wait_ge(ready, base + k + 1)
                    last = three_passes(s, lambda w: w[:, u, k * P:(k + 1) * P], hi, lo, k, KT, middle)
                    if k == KT - 1:
                        last.then_inc(unit_done, 1)
                    if between:
                        between(k)
                jobs.take_unit()

            def project_pair(hi, lo, ready, base=0, between=None):
                s, u = open_slot(), jobs.unit.n % 2
                pe.wait_ge(slot_free[1 - s], jobs.used(1))
                pe.wait_ge(w_split, jobs.unit(2))
                for k in range(KT):
                    pe.wait_ge(ready, base + k + 1)
                    for n in range(2):
                        v = (u + n) % 2
                        last = three_passes((s + n) % 2, lambda w: w[:, v, k * P:(k + 1) * P], hi, lo, k, KT)
                        if k == KT - 1:
                            last.then_inc(unit_done, 1)
                    if between:
                        between(k)
                jobs.take_unit()
                jobs.take_unit()

            def down():
                pe.wait_ge(hid_ready, hid())
                for half in range(2):
                    u = jobs.unit.n % 2
                    pe.wait_ge(w_split, jobs.unit(1))
                    for m in range(4):
                        s = open_slot()
                        for k in range(2):
                            last = three_passes(s, lambda w: w[:, u, k * 512 + m * P:k * 512 + (m + 1) * P],
                                                hid_hi, hid_lo, k, 2)
                        if m < 3:
                            last.then_inc(part_done, 1)
                            jobs.take_part()
                        else:
                            last.then_inc(unit_done, 1)
                            jobs.take_unit()

            def modulate_tile(bank, j):
                if j == 0 and (batch.turn is not None or batch.n >= 2):
                    pe.wait_ge(ada_free, batch(-1 if batch.turn is None else 0))
                b = bank_y if bank == "y" else bank_x
                pe.wait_ge(ada_in[j], (batch() + 1) * 16)
                for k in range(KT):
                    last = pe.matmul(b[:, 16 * j:16 * j + NV], ada[:, j, k * P:(k + 1) * P], cs[:, k, :],
                                     start=(k == 0), stop=(k == KT - 1))
                last.then_inc(ada_used, 1)
                if j == AB - 1:
                    batch.add()

            def modulate(bank):
                for j in range(AB):
                    modulate_tile(bank, j)

            def reduce_features(src, ready, value):
                s = open_slot()
                pe.wait_ge(ready, value)
                for g, (a, b) in enumerate(GROUPS):
                    last = pe.matmul(slots[:, s, g, 0:b - a], mean[:], src[:, a:b], start=True, stop=True)
                last.then_inc(part_done, 1)
                jobs.take_part()

            def ffn(p, ada_too):
                def early(n):
                    return (lambda k: modulate_tile("xy"[n % 2], k // 2) if k % 2 else None) if ada_too else None

                project_pair(u_hi, u_lo, h_ready, p * KT, (lambda k: modulate_tile("xy"[k // 4], k % 4)) if ada_too else None)
                project(u_hi, u_lo, between=early(2))
                project(u_hi, u_lo, between=early(3))
                hid.add(2)
                extra = [(batch, 1)] if ada_too else []
                with repeat(pe, FG - 1, *jobs.per(12, 6, 6), (hid, 2), *extra):
                    for j in range(4):
                        project(u_hi, u_lo)
                        if ada_too:
                            modulate_tile("x", j)
                        if j == 1:
                            down()
                            hid.add(2)
                down()

            pe.wait_ge(cs_ready, 1)
            for n in range(4):
                if n == 3:
                    pe.wait_ge(consts_ready, 1)
                    reduce_features(ss, sq_added, KT)
                modulate("xy"[n % 2])
            ffn(0, True)

            reduce_features(ss, sq_added, 2 * KT)
            s = open_slot()
            pe.wait_ge(wg_ready, 1)
            pe.wait_ge(slot_free[1 - s], jobs.used(1))
            pe.wait_ge(w_split, jobs.unit(1))
            u = jobs.unit.n % 2
            for k in range(KT):
                pe.wait_ge(h_ready, KT + k + 1)
                for q, (w, r) in enumerate(((wg_hi, u_hi), (wg_hi, u_lo), (wg_lo, u_hi))):
                    for g, (a, b) in enumerate(GROUPS):
                        last = pe.matmul(slots[0:36, s, g, 0:b - a], w[:, k, :], r[:, k, a:b],
                                         start=(k == 0 and q == 0), stop=(k == KT - 1 and q == 2))
                if k == KT - 1:
                    last.then_inc(part_done, 1)
                last = three_passes(1 - s, lambda w: w[:, u, k * P:(k + 1) * P], u_hi, u_lo, k, KT)
            last.then_inc(unit_done, 1)
            jobs.take_part()
            jobs.take_unit()
            for _ in range(3):
                project(u_hi, u_lo)
            pe.wait_ge(rows_dve, 4)
            pe.wait_ge(rows_act, 4)
            pe.wait_ge(ada_free, batch.n)
            pe.wait_ge(tables, 5)
            for n in range(4):
                bank, full, free, use = ((bank_x, x_full, x_free, xu), (bank_y, y_full, y_free, yu))[n % 2]
                if n >= 2:
                    pe.wait_ge(free, use())
                for j in range(4):
                    if n < 2:
                        c = 4 * n + j
                        last = pe.transpose(bank[:, j * P:(j + 1) * P], rows[:, ROW_Q, c * CH:(c + 1) * CH], ident[:])
                    else:
                        a = NP + (4 * (n - 2) + j) * TB
                        last = pe.matmul(bank[0:TB, j * P:(j + 1) * P], rows[:, ROW_Q, a:a + TB], ident[:],
                                         start=True, stop=True)
                last.then_inc(full, 1)
                use.add()

            q_of = lambda m, a, n: qkvo[:, m, a:a + n]
            k_of = lambda m, a, n: qkvo[:, 2 + m, a:a + n]
            v_of = lambda m, a, n: qkvo[:, 4 + m, a:a + n]

            def piece(kind, i, stage):
                if i < 0:
                    return
                a, L = seg(kind, i)
                mem = c_cur if kind == "p" else st[:, i % 3]
                if stage == 0:
                    pe.wait_ge(y_free, yu())
                    for m in range(2):
                        pe.matmul(bank_y[0:L, 0:L], k_of(m, a, L), q_of(m, a, L), start=(m == 0), stop=(m == 1))
                    pe.matmul(bank_y[0:L, P:P + L], ones[:, 0:L], g_cur[:, a:a + L], start=True, stop=False)
                    pe.matmul(bank_y[0:L, P:P + L], ident[0:L, 0:L], mask[0:L, 0:L], start=False, stop=True).then_inc(y_full, 1)
                pe.wait_ge(x_free, xu())
                if stage == 0:
                    for n, src in enumerate((k_of(0, a, L), k_of(1, a, L), v_of(0, a, L), v_of(1, a, L))):
                        if kind == "p":
                            last = pe.transpose(bank_x[0:L, n * P:(n + 1) * P], src, ident[:])
                        else:
                            last = pe.matmul(bank_x[0:L, n * P:(n + 1) * P], src, ident[:], start=True, stop=True)
                    last.then_inc(x_full, 1)
                elif stage == 1:
                    if kind == "s":
                        pe.wait_ge(st_in[i % 3], 16 * sts[i % 3].add())
                        pe.wait_ge(y_free, yu())
                    for m in range(2):
                        last = pe.matmul(bank_x[0:L, 0:C1], q_of(m, a, L), mem[:, m, :], start=(m == 0), stop=(m == 1))
                    last.then_inc(x_full, 1)
                    if kind == "p":
                        pe.wait_ge(y_free, yu())
                    pe.matmul(bank_y[0:L, 0:C1], dw[0:L, 0:L], vaug[0:L, :], start=True, stop=True).then_inc(y_full, 1)
                elif stage == 2:
                    pe.matmul(bank_x[:, 0:C1], ktok[0:L, 0:P], vws[0:L, :], start=True, stop=True).then_inc(x_full, 1)
                    pe.wait_ge(y_free, yu())
                    pe.matmul(bank_y[:, 0:C1], ktok[0:L, P:HD], vws[0:L, :], start=True, stop=True).then_inc(y_full, 1)
                else:
                    pe.wait_ge(hs_ready, steps.add())
                    for m in range(2):
                        src, dst = hs_of[kind][0:L, m * P:(m + 1) * P], bank_x[:, m * P:m * P + L]
                        if kind == "p":
                            last = pe.transpose(dst, src, ident[:])
                        else:
                            last = pe.matmul(dst, src, ident[0:L, 0:L], start=True, stop=True)
                    last.then_inc(x_full, 1)
                xu.add()
                if stage < 3:
                    yu.add()

            def section_a():
                for _ in range(8):
                    project(u_hi, u_lo)

            def section_b(n_units):
                s, written = jobs.slot(), (jobs.used(0), jobs.used(1))

                def first():
                    for more in (0, 1):
                        pe.wait_ge(slot_free[(s + more) % 2], written[more])
                    pe.wait_ge(head_ready, heads.add())
                    pe.wait_ge(x_free, xu())
                    pe.matmul(bank_x[:, 0:NC + NB], ones[:], apm[:], start=True, stop=True).then_inc(x_full, 1)
                    xu.add()

                for n in range(n_units):
                    def between(k):
                        if n * KT + k == LEAD * n_units // 8 - 1:
                            first()
                        here = pieces_at(n_units, n, k)
                        for q in here[len(here) // 2:]:
                            piece(*q)

                    def middle(k):
                        here = pieces_at(n_units, n, k)
                        for q in here[:len(here) // 2]:
                            piece(*q)
                    project(u_hi, u_lo, between=between, middle=middle)
                piece("p", NC - 1, 3)
                piece("s", NB - 1, 3)

            sx = [(sts[0], 3), (sts[1], 3), (sts[2], 2)]
            with repeat(pe, H - 1, *jobs.per(16, 16, 0), (xu, 65), (yu, 48), (steps, 16), (heads, 1), *sx):
                section_a()
                section_b(8)
            section_a()
            section_b(4)

            for m in range(1, KT):
                if m == 1:
                    project_pair(u_hi, u_lo, b_ready)
                else:
                    project(u_hi, u_lo)
                if m == MEANS_AFTER[0]:
                    reduce_features(a_tmp[:, 5], y_cent, 1)
                if m == MEANS_AFTER[1]:
                    reduce_features(b_cur[:, 0], ysq_added, KT)
            for m in range(KT):
                project(a_hi, a_lo, a_ready if m == 0 else None)
            project_pair(u_hi, u_lo, z_ready)
            for m in range(KT - 2):
                project(u_hi, u_lo)
            reduce_features(ss, sq_added, 3 * KT)
            ffn(2, False)
            reduce_features(ss, sq_added, 4 * KT)

        @block.scalar
        def _(act):
            jobs = Jobs()
            sqs = Tally()
            xu, yu = Tally(), Tally()
            steps = Tally()
            outs = [Tally(1), Tally(1)]

            def squares(p):
                for k in range(KT):
                    if p > 0:
                        act.wait_ge(x_final, (p - 1) * KT + k + 1)
                    else:
                        act.wait_ge(x_tile[k], 16)
                        if k == 0:
                            act.wait_ge(x_in, 16)
                    if sqs.n >= 2:
                        act.wait_ge(sq_added, sqs(-1))
                    act.activation(sq[k % 2][:, 0:NT], x[:, k, 0:NT], ACT.Square).then_inc(sq_done, 1)
                    sqs.add()

            def root(dst):
                s, done, _ = jobs.take_part()
                act.wait_ge(part_done, done)
                act.activation(tile3(dst), bank3(s), ACT.Sqrt, bias=eps[:, 0:1]).then_inc(slot_free[s], 1)

            def norm(p):
                squares(p)
                root(rstd)
                sh = mods[:, 3 * p * KT:(3 * p + 1) * KT, :]
                for k in range(KT):
                    act.wait_ge(t_ready, p * KT + k + 1)
                    act.activation(u_hi[:, k, 0:NP], tn[k % 2][:, 0:NP], ACT.Identity, bias=sh[:, k, 0:1])
                    act.activation(u_hi[:, k, NP:NT], tn[k % 2][:, NP:NT], ACT.Copy).then_inc(hi_ready, 1)

            def ffn():
                def gate():
                    s, done, _ = jobs.take_unit()
                    act.wait_ge(unit_done, done)
                    act.activation(tile3(sg), bank3(s), ACT.Silu).then_inc(slot_free[s], 1)

                def high(j, up):
                    act.wait_ge(slot_free[up[0]], up[2])
                    act.activation(hid_hi[:, j, :], prod, ACT.Copy).then_inc(hid_hi_done, 1)

                for j in range(2):
                    gate()
                    high(j, jobs.take_unit())
                with repeat(act, FG - 1, *jobs.per(12, 6, 6)):
                    gate()
                    up = jobs.take_unit()
                    for _ in range(2):
                        for _ in range(3):
                            jobs.take_part()
                        _, done, _ = jobs.take_unit()
                    act.wait_ge(unit_done, done)
                    high(0, up)
                    gate()
                    high(1, jobs.take_unit())
                for _ in range(2):
                    for _ in range(3):
                        jobs.take_part()
                    jobs.take_unit()

            act.wait_ge(c_in, 16)
            act.activation(cs[:], cs[:], ACT.Silu).then_inc(cs_ready, 1)
            act.wait_ge(consts_ready, 1)
            norm(0)
            ffn()
            norm(1)

            act.wait_ge(consts_in, 16 * 7)
            s, done, _ = jobs.take_part()
            act.wait_ge(part_done, done)
            act.wait_ge(rows_dve, 1)
            act.activation(tile3(rows[0:4, ROW_I, :]), slots[0:4, s, :, 0:GW], ACT.Identity, bias=b_if[0:4, 0:1])
            act.activation(tile3(rows[0:4, ROW_Z, :]), slots[32:36, s, :, 0:GW], ACT.Identity,
                           bias=b_if[32:36, 0:1]).then_inc(slot_free[s], 1)
            act.drain()
            act.activation(rows[0:4, ROW_E, :], rows[0:4, ROW_Z, :], ACT.Abs)
            act.drain()
            act.activation(rows[0:4, ROW_E, :], rows[0:4, ROW_E, :], ACT.Exp, scale=-1.0)
            act.drain()
            act.activation(rows[0:4, ROW_E, :], rows[0:4, ROW_E, :], ACT.Ln, bias=1.0).then_inc(rows_act, 1)

            def gate_tile(n, bias):
                s, done, _ = jobs.take_unit()
                act.wait_ge(unit_done, done)
                act.activation(tile3(n), bank3(s), ACT.Tanh, bias=bias, scale=0.5).then_inc(slot_free[s], 1)

            def rows_to_exp():
                act.wait_ge(rows_dve, 2)
                act.activation(rows[32:36, ROW_Q, 0:NT], rows[0:4, ROW_I, 0:NT], ACT.Exp).then_inc(rows_act, 1)
                act.activation(rows[64:68, ROW_Q, 0:NT], rows[0:4, ROW_Z, 0:NT], ACT.Exp, scale=-1.0).then_inc(rows_act, 1)
                act.wait_ge(rows_dve, 3)
                act.activation(rows[96:100, ROW_Q, 0:NT], rows[0:4, ROW_T, 0:NT], ACT.Exp).then_inc(rows_act, 1)
                act.wait_ge(m_ready, 1)
                act.dma_start(t_out["m"], m_fin[:]).then_inc(m_out, 16)

            def conv_gate(h1, t):
                if outs[t].turn is not None:
                    act.wait_ge(th_out[t], 16 * outs[t]())
                gate_tile(th[:, t, :], bias_of(h1, 8 + 2 * t))

            act.wait_ge(biases_ready, 1)
            conv_gate(0, 0)
            rows_to_exp()
            jobs.take_unit()
            conv_gate(0, 1)
            jobs.take_unit()

            def section_a(h):
                for j in range(8):
                    if j >= 6:
                        gate_tile(qkvo[:, j, :], bias_of(h, j))
                        act.drain()
                        last = act.activation(qkvo[:, j, :], qkvo[:, j, :], ACT.Identity, bias=1.0)
                        if j == 7:
                            last.then_inc(o_ready, 1)
                        continue
                    s, done, _ = jobs.take_unit()
                    act.wait_ge(unit_done, done)
                    act.activation(tile3(qkvo[:, j, :]), bank3(s), ACT.Identity, bias=bias_of(h, j),
                                   scale=HD ** -0.5 if j < 2 else 1.0).then_inc(slot_free[s], 1)

            def piece(h, kind, i, stage):
                if i < 0:
                    return
                _, L = seg(kind, i)
                c = col_h[:, i, :] if kind == "p" else cols_h[:, i, :]
                if stage == 0:
                    act.wait_ge(y_full, yu.add())
                    act.activation(dw[0:L, 0:L], bank_y[0:L, P:P + L], ACT.Exp, bias=c[0:L, 0:1]).then_inc(d_ready, 1)
                    act.wait_ge(x_full, xu.add())
                    act.activation(vaug[0:L, 0:HD], bank_x[0:L, HD:2 * HD], ACT.Copy)
                    act.activation(ktok[0:L, :], bank_x[0:L, 0:HD], ACT.Copy)
                    act.activation(vws[0:L, 0:HD], bank_x[0:L, HD:2 * HD], ACT.Copy, scale=c[0:L, 3:4]).then_inc(x_free, 1)
                elif stage == 1:
                    act.wait_ge(x_full, xu.add())
                    act.activation(tin[0:L, :], bank_x[0:L, 0:C1], ACT.Copy, scale=c[0:L, 1:2]).then_inc(x_free, 1)
                    yu.add()
                elif stage == 2:
                    act.wait_ge(rd_ready, steps.add())
                    e = "ps".index(kind)
                    act.activation(tin[0:L, 0:HD], hn_of[kind][0:L, 0:HD], ACT.Square, scale=inv_den[0:L, e:e + 1],
                                   accum_out=sq_sum[0:L, e:e + 1]).then_inc(r_ready, 1)
                    xu.add()
                    yu.add()
                else:
                    xu.add()

            def section_b(h, n_units):
                xu.add()
                for n in range(n_units):
                    for q in pieces_at(n_units, n):
                        piece(h, *q)
                    if n_units == 8 and n < 4:
                        if n % 2:
                            jobs.take_unit()
                        else:
                            conv_gate(h + 1, n // 2)
                        continue
                    j = n - (n_units - 4)
                    t = j % 2
                    act.wait_ge(th_out[t], 16 * outs[t]())
                    gate_tile(th[:, t, :], bias_of(h, 12 + j))
                    outs[t].add()
                piece(h, "p", NC - 1, 3)
                piece(h, "s", NB - 1, 3)

            sx = [(outs[0], 2), (outs[1], 2)]
            xu.add(2)
            yu.add(2)
            act.wait_ge(x_out, 16)
            with repeat(act, H - 1, *jobs.per(16, 16, 0), (xu, 65), (yu, 48), (steps, 16), *sx) as h:
                section_a(h)
                section_b(h, 8)
            section_a(H - 1)
            section_b(H - 1, 4)

            for k in range(KT):
                if k < 6:
                    act.wait_ge(b_back[k], 16)
                elif k == 6:
                    act.wait_ge(x_free, xu.n)
                act.activation(u_hi[:, k, :], b_tiles[k], ACT.Copy).then_inc(b_hi_done, 1)
            for k in range(KT):
                act.wait_ge(y_cent, k + 2)
                if k >= 2:
                    act.wait_ge(ysq_added, k - 1)
                act.activation(a_tmp[:, 6 + k % 2, 0:NT], y[:, k, 0:NT], ACT.Square).then_inc(ysq_done, 1)
            for _ in range(2):
                jobs.take_unit()
            jobs.take_part()
            for _ in range(3):
                jobs.take_unit()
            root(b_cur[:, 0, :])
            for k in range(KT):
                act.wait_ge(y_norm, k + 1)
                act.activation(y[:, k, :], y[:, k, :], ACT.Silu, bias=vecs[:, LN_B, k:k + 1],
                               scale=vecs[:, LN_G, k:k + 1])
                act.drain()
                act.activation(a_hi[:, k, :], y[:, k, :], ACT.Copy).then_inc(a_hi_done, 1)
            for _ in range(3):
                jobs.take_unit()
            for k in range(KT):
                jobs.take_unit()
                act.wait_ge(z_done, k + 1)
                act.activation(u_hi[:, k, :], z[:, k, :], ACT.Copy).then_inc(z_hi_done, 1)
            for _ in range(KT):
                jobs.take_unit()
            norm(2)
            ffn()
            squares(3)
            root(rstd)

        @block.vector
        def _(dve):
            jobs = Jobs()
            batch, prods, sqs = Tally(), Tally(), Tally()
            xu, yu, steps, heads = Tally(), Tally(), Tally(), Tally()

            def stt(out, in0, scalar, in1, op0, op1):
                return dve.scalar_tensor_tensor(out=out, in0=in0, scalar=scalar, in1=in1, op0=op0, op1=op1)

            def ada_evac(bank):
                batch.add()
                dve.wait_ge(ada_used, batch() * AB)
                b = (bank_x if bank == "x" else bank_y)[:, 0:16 * AB].rearrange("p (j n) -> p j n", j=AB)[:, :, 0:NV]
                if batch.turn is None:
                    n = (batch.n - 1) * AB
                    dst, bias = mods[:, n:n + AB, :], b_ada[:, n:n + AB]
                else:
                    n = batch(-1) * AB
                    dst, bias = mods[:, bass.ds(n, AB), :], b_ada[:, bass.ds(n, AB)]
                dve.tensor_tensor(dst, b, bias.unsqueeze(2).to_broadcast([P, AB, NV]), ALU.add).then_inc(ada_free, 1)

            def derive_norm(p, gain):
                stt(m_a[:, p], mods[:, (3 * p + 1) * KT:(3 * p + 2) * KT, :], 1.0,
                    vecs[:, gain, :].unsqueeze(2).to_broadcast([P, KT, NV]), ALU.add, ALU.mult)

            def derive_gate(p):
                dve.tensor_scalar(m_g[:, p], mods[:, (3 * p + 2) * KT:(3 * p + 3) * KT, :], 0.5, None, ALU.mult)

            def sum_tile(k):
                dve.drain()
                dve.wait_ge(sq_done, sqs.add())
                if k == 0:
                    last = dve.tensor_copy(ss[:, 0:NT], sq[0][:, 0:NT])
                else:
                    last = dve.tensor_tensor(ss[:, 0:NT], ss[:, 0:NT], sq[k % 2][:, 0:NT], ALU.add)
                last.then_inc(sq_added, 1)

            def reciprocal_of_root(after_sums=None):
                if after_sums:
                    after_sums()
                s, _, freed = jobs.take_part()
                dve.drain()
                dve.wait_ge(slot_free[s], freed)
                dve.reciprocal(rstd[:, 0:NT], rstd[:, 0:NT])
                dve.drain()

            def norm(p, after_sums=None, after_root=None):
                reciprocal_of_root(after_sums)
                if after_root:
                    after_root()
                sh = mods[:, 3 * p * KT:(3 * p + 1) * KT, :]

                def scaled(k):
                    t = tn[k % 2]
                    ts = sample3(t[:, NP:NT])
                    dve.drain()
                    dve.tensor_tensor(t[:, NP:NT], x[:, k, NP:NT], rstd[:, NP:NT], ALU.mult)
                    stt(t[:, 0:NP], x[:, k, 0:NP], m_a[:, p, k, 0:1], rstd[:, 0:NP], ALU.mult, ALU.mult)
                    dve.drain()
                    dve.tensor_tensor(ts, ts, per_batch(m_a[:, p, k, 1:NV]), ALU.mult)
                    dve.drain()
                    dve.tensor_tensor(ts, ts, per_batch(sh[:, k, 1:NV]), ALU.add).then_inc(t_ready, 1)

                def low(k):
                    t = tn[k % 2]
                    dve.wait_ge(hi_ready, p * KT + k + 1)
                    stt(u_lo[:, k, 0:NP], t[:, 0:NP], sh[:, k, 0:1], u_hi[:, k, 0:NP].bitcast(F32), ALU.add, ALU.subtract)
                    dve.tensor_tensor(u_lo[:, k, NP:NT], t[:, NP:NT], u_hi[:, k, NP:NT].bitcast(F32),
                                      ALU.subtract).then_inc(h_ready, 1)

                scaled(0)
                for k in range(1, KT):
                    scaled(k)
                    low(k - 1)
                dve.drain()
                low(KT - 1)

            def residual(s, p, m, final=None):
                g = m_g[:, p, m, :]
                dve.tensor_tensor(sample3(xs_tmp[:]), sample3(slots[:, s, 2, LP:LP + NB * TB]), per_batch(g[:, 1:NV]), ALU.mult)
                x01 = x[:, m, 0:2 * GW].rearrange("p (g n) -> p g n", g=2)
                stt(x01, slots[:, s, 0:2, 0:GW], g[:, 0:1], x01, ALU.mult, ALU.add)
                stt(x[:, m, 2 * GW:NP], slots[:, s, 2, 0:LP], g[:, 0:1], x[:, m, 2 * GW:NP],
                    ALU.mult, ALU.add).then_inc(slot_free[s], 1)
                dve.drain()
                last = dve.tensor_tensor(x[:, m, NP:NT], x[:, m, NP:NT], xs_tmp[:], ALU.add)
                if final is not None:
                    last.then_inc(final, 1)

            def ffn(p, ada_too, before_last=None):
                def product():
                    dve.drain()
                    s, _, freed = jobs.take_unit()
                    dve.wait_ge(slot_free[s], freed)
                    s, done, _ = jobs.take_unit()
                    dve.wait_ge(unit_done, done)
                    dve.tensor_tensor(tile3(prod), tile3(sg), bank3(s), ALU.mult).then_inc(slot_free[s], 1)
                    prods.add()

                def low(j):
                    dve.wait_ge(hid_hi_done, prods())
                    dve.tensor_tensor(hid_lo[:, j, :], prod, hid_hi[:, j, :].bitcast(F32), ALU.subtract).then_inc(hid_ready, 1)

                def down(final=None):
                    for m in range(KT):
                        dve.drain()
                        if m % 4 < 3:
                            s, done, _ = jobs.take_part()
                            dve.wait_ge(part_done, done)
                        else:
                            s, done, _ = jobs.take_unit()
                            dve.wait_ge(unit_done, done)
                        residual(s, p, m, final)
                        if final is not None and m:
                            sum_tile(m - 1)

                for j in range(2):
                    product()
                    if ada_too:
                        ada_evac("x")
                        ada_evac("y")
                    low(j)
                if ada_too:
                    dve.drain()
                    derive_gate(0)
                extra = [(batch, 1)] if ada_too else []
                with repeat(dve, FG - 1, *jobs.per(12, 6, 6), (prods, 2), *extra):
                    product()
                    down()
                    low(0)
                    product()
                    low(1)
                    if ada_too:
                        ada_evac("x")
                if before_last:
                    before_last()
                down(x_final)

            dve.memset(x[:, :, NT:W], 0.0)
            dve.memset(small[:], 0.0)
            dve.memset(slots[:], 0.0)
            dve.memset(mean[:], 1.0 / D)
            dve.memset(ones[:], 1.0)
            dve.memset(eps[:], EPS).then_inc(consts_ready, 1)
            dve.wait_ge(consts_in, 16 * 7)
            dve.tensor_scalar(b_in[:, :, 0:2], b_in[:, :, 0:2], HD ** -0.5, None, ALU.mult)
            dve.tensor_scalar(b_in[:, :, 6:8], b_in[:, :, 6:8], 0.5, None, ALU.mult)
            dve.tensor_scalar(b_in[:, :, 8:12:2], b_in[:, :, 8:12:2], 0.5, None, ALU.mult)
            dve.tensor_scalar(b_in[:, :, 12:16], b_in[:, :, 12:16], 0.5, None, ALU.mult)
            dve.tensor_scalar(vecs[:, MH, :], vecs[:, MH, :], 0.5, None, ALU.mult).then_inc(biases_ready, 1)

            ada_evac("x")
            ada_evac("y")

            def last_mods():
                ada_evac("x")
                ada_evac("y")
                dve.drain()
                derive_norm(0, NORM1)
                dve.drain()

            for k in range(KT):
                sum_tile(k)
            norm(0, after_root=last_mods)

            def derive_others():
                dve.drain()
                derive_norm(1, NORM2)
                derive_norm(2, NORM3)
                derive_gate(1)
                derive_gate(2)

            ffn(0, True, derive_others)

            dve.drain()
            dve.memset(wg_raw[:], 0.0).then_inc(wg_cleared, 1)
            sum_tile(KT - 1)

            def split_gate_weights():
                dve.wait_ge(gate_w_in, 32)
                dve.tensor_copy(wg_hi[:], wg_raw[:])
                dve.drain()
                dve.tensor_tensor(wg_lo[:], wg_raw[:], wg_hi[:].bitcast(F32), ALU.subtract).then_inc(wg_ready, 1)

            norm(1, split_gate_weights)

            def r(i, a=0, b=NT, p=0):
                return rows[p:p + 4, i, a:b]

            dve.memset(rows[:, ROW_Q, :], 0.0)
            dve.memset(rows[0:4, ROW_1, :], 1.0)
            dve.memset(mc[:], 0.0).then_inc(rows_dve, 1)
            dve.drain()
            jobs.take_part()
            dve.wait_ge(rows_act, 1)
            stt(r(ROW_Z), r(ROW_Z), 0.0, r(ROW_E), ALU.min, ALU.subtract)
            dve.drain()
            segs = [seg("p", i) for i in range(NC)] + [seg("s", i) for i in range(NB)]
            for a, L in segs:
                dve.tensor_tensor_scan(r(ROW_B, a, a + L), r(ROW_1, a, a + L), r(ROW_Z, a, a + L), 0.0, ALU.mult, ALU.add)
            dve.drain()
            dve.tensor_tensor(r(ROW_Q), r(ROW_I), r(ROW_B), ALU.subtract)
            dve.drain()
            for i, (a, L) in enumerate(segs):
                m0 = mc[:, i:i + 1] if i < NC else ms[:, i - NC:i - NC + 1]
                dve.tensor_tensor_scan(g_row[:, a:a + L], r(ROW_Q, a, a + L), r(ROW_Q, a, a + L), m0, ALU.max, ALU.max)
                if i < NC:
                    dve.drain()
                    dve.tensor_tensor(mc[:, i + 1:i + 2], g_row[:, a + L - 1:a + L], r(ROW_B, a + L - 1, a + L), ALU.add)
                    dve.drain()
            dve.drain()
            dve.tensor_copy(m_fin[:, 0:1], mc[:, NC:NC + 1])
            dve.tensor_tensor(m_fin[:, 1:1 + NB], g_row[:, NP + TB - 1:NT:TB], r(ROW_B, NP + TB - 1, NT)[:, ::TB], ALU.add).then_inc(m_ready, 1)
            gp = g_row[:, 0:NP].rearrange("p (c l) -> p c l", c=NC)
            gs = g_row[:, NP:NT].rearrange("p (c l) -> p c l", c=NB)

            def rp(i):
                return r(i, 0, NP).rearrange("p (c l) -> p c l", c=NC)

            def rs(i):
                return r(i, NP, NT).rearrange("p (c l) -> p c l", c=NB)

            dve.tensor_tensor(rp(ROW_I), mc[:, 0:NC].unsqueeze(2).to_broadcast([4, NC, CH]), gp, ALU.subtract)
            dve.tensor_tensor(rs(ROW_I), ms[:].unsqueeze(2).to_broadcast([4, NB, TB]), gs, ALU.subtract)
            dve.tensor_tensor(r(ROW_Z), r(ROW_B), g_row[:], ALU.add).then_inc(rows_dve, 1)
            dve.tensor_tensor(rp(ROW_T), rp(ROW_Q), gp[:, :, CH - 1:CH].to_broadcast([4, NC, CH]), ALU.subtract)
            dve.tensor_tensor(rs(ROW_T), rs(ROW_Q), gs[:, :, TB - 1:TB].to_broadcast([4, NB, TB]), ALU.subtract).then_inc(rows_dve, 1)
            dve.wait_ge(rows_act, 2)
            dve.tensor_copy(apv[:, 0:NC], rows[32:36, ROW_Q, CH - 1:NP:CH])
            dve.tensor_copy(apv[:, NC:NC + NB], rows[32:36, ROW_Q, NP + TB - 1:NT:TB]).then_inc(rows_dve, 1)

            def conv_gate(t):
                s, _, freed = jobs.take_unit()
                dve.drain()
                dve.wait_ge(slot_free[s], freed)
                dve.tensor_scalar(th[:, t, :], th[:, t, :], 0.5, 0.5, ALU.mult, ALU.add)

            def conv_value(h1, t):
                dve.drain()
                s, done, _ = jobs.take_unit()
                dve.wait_ge(unit_done, done)
                convs[t].add(2)
                b = bias_of(h1, 9 + 2 * t)
                stt(glu[:, t, PAST:PAST + 2 * GW].rearrange("p (g n) -> p g n", g=2), slots[:, s, 0:2, 0:GW], b,
                    th[:, t, 0:2 * GW].rearrange("p (g n) -> p g n", g=2), ALU.add, ALU.mult)
                stt(glu[:, t, PAST + 2 * GW:PAST + NP], slots[:, s, 2, 0:LP], b, th[:, t, 2 * GW:NP], ALU.add, ALU.mult)
                stt(glus[:, t, :, PAST:PAST + TB], sample3(slots[:, s, 2, LP:LP + NB * TB]), b,
                    sample3(th[:, t, NP:NT]), ALU.add, ALU.mult).then_inc(slot_free[s], 1)

            convs = [Tally(), Tally()]
            dve.memset(glu[:, :, 0:PAST], 0.0)
            conv_gate(0)
            conv_value(0, 0)
            conv_gate(1)
            conv_value(0, 1)

            for n in range(4):
                bank, full, free, use = ((bank_x, x_full, x_free, xu), (bank_y, y_full, y_free, yu))[n % 2]
                dve.wait_ge(full, use.add())
                L = P if n < 2 else TB
                dst = (col if n < 2 else cols)[:, 4 * (n % 2):4 * (n % 2) + 4, :]
                src = bank[0:L].rearrange("p (c q e) -> p c q e", c=4, q=4)[:, :, :, 0:4]
                dve.tensor_copy(dst.rearrange("p c (q h) -> p c q h", q=4), src).then_inc(free, 1)
            dve.memset(y[:, :, NT:W], 0.0)
            dve.memset(vaug[:, HD:C1], 1.0)
            dve.memset(b_cur[:, :, NT:W], 0.0).then_inc(b_out, 16)
            dve.memset(c_cur[:], 0.0).then_inc(c_out, 16)
            for n in range(3):
                dve.memset(st[:, n], 0.0).then_inc(st_out[n], 16)
            for t in range(2):
                dve.memset(th[:, t, NT:W], 0.0).then_inc(th_out[t], 16)
            dve.drain()

            def prelude(h):
                of_head = (lambda t, n: t[:, :, h:16:4]) if isinstance(h, int) else (
                    lambda t, n: t.rearrange("p c (q h) -> p c q h", q=4)[:, :, :, bass.ds(h, 1)].rearrange("p c q h -> p c (q h)"))
                sel = ident[0:4, h:h + 1] if isinstance(h, int) else ident[0:4, bass.ds(h, 1)]
                dve.drain()
                dve.wait_ge(c_out, 16 * heads(1))
                dve.wait_ge(b_out, 16 * heads(1))
                dve.tensor_copy(col_h[:], of_head(col[:], NC))
                dve.tensor_copy(cols_h[:], of_head(cols[:], NB))
                dve.tensor_scalar(g_cur[:], g_row[:], sel, -1.0, ALU.mult, ALU.mult)
                dve.tensor_scalar(apm[:], apv[:], sel, None, ALU.mult)
                dve.memset(c_cur[:], 0.0).then_inc(head_ready, 1)
                heads.add()

            def taps(h):
                tiles = [2 * h, 2 * h + 1]
                pick = lambda t: (y[:, tiles[t], :] if isinstance(h, int) else y[:, bass.ds(tiles[t], 1), :].rearrange("p a n -> p (a n)"))
                if isinstance(h, int):
                    dve.tensor_copy(dw_cur[:], w_dw[:, 2 * h:2 * h + 2, :])
                else:
                    dve.tensor_copy(dw_cur[:], w_dw[:, bass.ds(2 * h, 2), :])
                for j in range(CW):
                    if j == CW // 2:
                        prelude(h)
                    dve.drain()
                    if j == 0:
                        dve.wait_ge(glus_in, 32 * heads(1))
                        for t in range(2):
                            dve.wait_ge(conv_out[t], 16 * convs[t]())
                    for t in range(2):
                        yt = pick(t)
                        w = dw_cur[:, t, j:j + 1]
                        for out, src in ((yt[:, 0:NP], glu[:, t, j:j + NP]),
                                         (sample3(yt[:, NP:NT]), glus[:, t, :, j:j + TB])):
                            if j == 0:
                                b = vecs[:, B_DW, 2 * h + t:2 * h + t + 1] if isinstance(h, int) else vecs[:, B_DW, bass.ds(2 * h + t, 1)]
                                last = dve.tensor_scalar(out, src, w, b, ALU.mult, ALU.add)
                            else:
                                last = stt(out, src, w, out, ALU.mult, ALU.add)
                last.then_inc(taps_done, 1)

            def section_a(h):
                taps(h)
                for _ in range(8):
                    jobs.take_unit()

            def normalise():
                dve.wait_ge(r_ready, steps())
                dve.tensor_scalar(half_ms[:], sq_sum[:], 0.5 / HD, 0.5 * EPS, ALU.mult, ALU.add)
                dve.drain()
                dve.tensor_scalar(inv_rms[:].bitcast(I32), half_ms[:].bitcast(I32), -0.5, ROOT_BITS, ALU.mult, ALU.add)
                dve.drain()
                for _ in range(3):
                    dve.tensor_tensor(tmp_rms[:], inv_rms[:], inv_rms[:], ALU.mult)
                    dve.drain()
                    dve.tensor_tensor(tmp_rms[:], tmp_rms[:], half_ms[:], ALU.mult)
                    dve.drain()
                    stt(inv_rms[:], tmp_rms[:], 1.5, inv_rms[:], ALU.subtract, ALU.mult)
                    dve.drain()
                for e, kind in enumerate("ps"):
                    _, L = seg(kind, 0)
                    dve.tensor_scalar(hs_of[kind][0:L, :], hn_of[kind][0:L, 0:HD], inv_den[0:L, e:e + 1],
                                      inv_rms[0:L, e:e + 1], ALU.mult, ALU.mult).then_inc(hs_ready, 1)

            def piece(h, kind, i, stage):
                if i < 0:
                    return
                a, L = seg(kind, i)
                c = col_h[:, i, :] if kind == "p" else cols_h[:, i, :]
                mem = c_cur if kind == "p" else st[:, i % 3]
                if stage == 0:
                    xu.add()
                    dve.wait_ge(d_ready, steps.add())
                    yu.add()
                    dve.tensor_copy(vws[0:L, HD:C1], c[0:L, 3:4])
                    dve.tensor_tensor(dw[0:L, 0:L], bank_y[0:L, 0:L], dw[0:L, 0:L], ALU.mult).then_inc(y_free, 1)
                elif stage == 1:
                    dve.drain()
                    dve.wait_ge(y_full, yu.add())
                    dve.wait_ge(x_free, xu.add())
                    hn, e = hn_of[kind], "ps".index(kind)
                    dve.tensor_tensor(hn[0:L, :], bank_y[0:L, 0:C1], tin[0:L, :], ALU.add).then_inc(y_free, 1)
                    dve.drain()
                    stt(den[0:L, e:e + 1], hn[0:L, HD:C1], -1.0, hn[0:L, HD:C1], ALU.mult, ALU.max)
                    dve.drain()
                    dve.tensor_tensor(den[0:L, e:e + 1], den[0:L, e:e + 1], c[0:L, 2:3], ALU.max)
                    dve.drain()
                    dve.reciprocal(inv_den[0:L, e:e + 1], den[0:L, e:e + 1]).then_inc(rd_ready, 1)
                elif stage == 2:
                    ap = ap_h[:, i:i + 1] if kind == "p" else ap_h[:, NC + i:NC + i + 1]
                    for m, (bank, full, free, use) in enumerate(((bank_x, x_full, x_free, xu), (bank_y, y_full, y_free, yu))):
                        dve.wait_ge(full, use.add())
                        stt(mem[:, m, :], mem[:, m, :], ap, bank[:, 0:C1], ALU.mult, ALU.add).then_inc(free, 1)
                    if kind == "s":
                        normalise()
                else:
                    dve.wait_ge(x_full, xu.add())
                    for m in range(2):
                        g = vecs[:, MH, 2 * h + m:2 * h + m + 1] if isinstance(h, int) else vecs[:, MH, bass.ds(2 * h + m, 1)]
                        last = stt(b_cur[:, m, a:a + L], bank_x[:, m * P:m * P + L], g, qkvo[:, 6 + m, a:a + L], ALU.mult, ALU.mult)
                    last.then_inc(x_free, 1)
                    dve.drain()

            def section_b(h, n_units):
                dve.drain()
                dve.wait_ge(o_ready, heads())
                dve.wait_ge(x_full, xu.add())
                dve.tensor_copy(ap_h[:], bank_x[:, 0:NC + NB]).then_inc(x_free, 1)
                dve.drain()
                for n in range(n_units):
                    for q in pieces_at(n_units, n):
                        piece(h, *q)
                    if n_units == 8 and n < 4:
                        if n % 2 == 0:
                            conv_gate(n // 2)
                        else:
                            conv_value(h + 1, n // 2)
                    else:
                        jobs.take_unit()
                piece(h, "p", NC - 1, 3)
                piece(h, "s", NB - 1, 3)

            with repeat(dve, H - 1, *jobs.per(16, 16, 0), (xu, 65), (yu, 48), (steps, 16), (heads, 1), (convs[0], 2), (convs[1], 2)) as h:
                section_a(h)
                section_b(h, 8)
            section_a(H - 1)
            section_b(H - 1, 4)

            for k in range(KT):
                dve.wait_ge(b_hi_done, k + 1)
                dve.tensor_tensor(u_lo[:, k, :], b_tiles[k], u_hi[:, k, :].bitcast(F32), ALU.subtract).then_inc(b_ready, 1)
            ysum, yss = a_tmp[:, 5], b_cur[:, 0]
            dve.drain()
            for k in range(1, KT):
                last = dve.tensor_tensor(ysum, y[:, 0, :] if k == 1 else ysum, y[:, k, :], ALU.add)
                if k == KT - 1:
                    last.then_inc(y_cent, 1)
                dve.drain()

            for n in range(3):
                dve.wait_ge(st_out[n], 16 * [13, 13, 9][n])
            dve.wait_ge(c_out, 16 * (H + 1))
            for t in range(2):
                dve.wait_ge(conv_out[t], 16 * KT)

            def gated(n):
                m = n % KT
                s, done, _ = jobs.take_unit()
                dve.wait_ge(unit_done, done)
                dve.wait_ge(g_back[n % 2], 16 * (n // 2 + 1))
                if n < KT:
                    stt(tile3(z[:, m, :]), tile3(th[:, n % 2, :]), 1.0, bank3(s), ALU.add, ALU.mult).then_inc(slot_free[s], 1)
                else:
                    dve.drain()
                    stt(tile3(th[:, n % 2, :]), tile3(th[:, n % 2, :]), 1.0, bank3(s), ALU.add, ALU.mult).then_inc(slot_free[s], 1)
                    dve.drain()
                    dve.tensor_tensor(z[:, m, :], z[:, m, :], th[:, n % 2, :], ALU.add).then_inc(z_done, 1)

            gated(0)
            gated(1)
            s, done, _ = jobs.take_part()
            dve.wait_ge(part_done, done)
            dve.tensor_copy(tile3(ysum), bank3(s)).then_inc(slot_free[s], 1)
            dve.drain()
            for k in range(KT):
                dve.tensor_tensor(y[:, k, :], y[:, k, :], ysum, ALU.subtract).then_inc(y_cent, 1)
                if k:
                    dve.drain()
                    dve.wait_ge(ysq_done, k)
                    if k == 1:
                        dve.tensor_copy(yss[:, 0:NT], a_tmp[:, 6, 0:NT]).then_inc(ysq_added, 1)
                    else:
                        dve.tensor_tensor(yss[:, 0:NT], yss[:, 0:NT], a_tmp[:, 6 + (k - 1) % 2, 0:NT], ALU.add).then_inc(ysq_added, 1)
                if k == 4:
                    gated(2)
            dve.drain()
            dve.wait_ge(ysq_done, KT)
            dve.tensor_tensor(yss[:, 0:NT], yss[:, 0:NT], a_tmp[:, 7, 0:NT], ALU.add).then_inc(ysq_added, 1)
            gated(3)
            gated(4)
            s, _, freed = jobs.take_part()
            dve.drain()
            dve.wait_ge(slot_free[s], freed)
            dve.reciprocal(yss, yss)
            dve.drain()

            def a_low(k):
                dve.wait_ge(a_hi_done, k + 1)
                dve.tensor_tensor(a_lo[:, k, :], y[:, k, :], a_hi[:, k, :].bitcast(F32), ALU.subtract).then_inc(a_ready, 1)

            for k in range(KT):
                dve.tensor_tensor(y[:, k, :], y[:, k, :], yss, ALU.mult).then_inc(y_norm, 1)
                if k:
                    a_low(k - 1)
                if k in (2, 5):
                    gated(5 + k // 3)
            a_low(KT - 1)
            gated(7)
            for n in range(KT, 2 * KT):
                gated(n)
                dve.wait_ge(z_hi_done, n - KT + 1)
                dve.tensor_tensor(u_lo[:, n - KT, :], z[:, n - KT, :], u_hi[:, n - KT, :].bitcast(F32), ALU.subtract).then_inc(z_ready, 1)
            for m in range(KT):
                dve.drain()
                s, done, _ = jobs.take_unit()
                dve.wait_ge(unit_done, done)
                dve.wait_ge(x_tile[m], 32)
                residual(s, 1, m, x_final)
                if m:
                    sum_tile(m - 1)
            sum_tile(KT - 1)
            norm(2)
            ffn(2, False)
            sum_tile(KT - 1)
            reciprocal_of_root()
            for k in range(KT):
                dve.drain()
                if k >= 4:
                    dve.wait_ge(out_done[k % 4], 16 * (k // 4))
                stt(work[:, 4 + k % 4, 0:NT], x[:, k, 0:NT], vecs[:, NORMF, k:k + 1], rstd[:, 0:NT],
                    ALU.mult, ALU.mult).then_inc(out_ready, 1)


def _tiles(w):
    n = w.shape[1] // P
    return w.reshape(KT, P, n, P).transpose(2, 1, 0, 3).reshape(n, P, D)


def _down(w):
    return w.reshape(FG, 2, P, 2, 512).transpose(0, 3, 2, 1, 4).reshape(FG, 2, P, D)


def _ffn_units(gate, up, down):
    g, u, d = _tiles(gate), _tiles(up), _down(down)
    out = [g[0], u[0], g[1], u[1]]
    for i in range(1, FG):
        out += [g[2 * i], u[2 * i], d[i - 1][0], d[i - 1][1], g[2 * i + 1], u[2 * i + 1]]
    return out + [d[FG - 1][0], d[FG - 1][1]]


def _mixer_units(w_in):
    cv, cg, q, k, v, o, ga, gb = (_tiles(w_in[:, i * D:(i + 1) * D]) for i in range(8))
    out = [cg[0], cv[0], cg[1], cv[1]]
    for h in range(H):
        a, b = 2 * h, 2 * h + 1
        out += [q[a], q[b], k[a], k[b], v[a], v[b], o[a], o[b]]
        if h < H - 1:
            out += [cg[a + 2], cv[a + 2], cg[b + 2], cv[b + 2]]
        out += [ga[a], ga[b], gb[a], gb[b]]
    return out


def kernel(**inputs):
    import concourse.bacc as bacc
    from concourse.bass_utils import run_bass_kernel_spmd

    a = {k: np.asarray(v) for k, v in inputs.items()}
    w_in = a["w_in"][0]
    units = (_ffn_units(a["w1_gate"][0], a["w1_up"][0], a["w1_down"][0]) + _mixer_units(w_in)
             + list(_tiles(a["w_mlstm_out"][0])) + list(_tiles(a["w_conv_out"][0])) + list(_tiles(a["w_out"][0]))
             + _ffn_units(a["w2_gate"][0], a["w2_up"][0], a["w2_down"][0]))
    cv, cg, q, k, v, o, ga, gb = a["b_in"][0, :8 * D].reshape(8, H, 2, P)
    b_in = np.stack([q[:, 0], q[:, 1], k[:, 0], k[:, 1], v[:, 0], v[:, 1], o[:, 0], o[:, 1],
                     cg[:, 0], cv[:, 0], cg[:, 1], cv[:, 1], ga[:, 0], ga[:, 1], gb[:, 0], gb[:, 1]], 1)
    vecs = np.stack([a["norm_ffn1"][0], a["norm_mix"][0], a["norm_ffn2"][0], a["final_norm"], a["b_dw"][0],
                     a["ln_conv_g"][0], a["ln_conv_b"][0], a["mh_norm"][0].reshape(D)])
    state = np.concatenate([a["state_C"][0].transpose(1, 0, 3, 2).reshape(H, NB, 2, P, HD),
                            a["state_n"][0].transpose(1, 0, 2).reshape(H, NB, 2, P, 1)], -1)
    feats = {
        "w_units": np.stack(units),
        "ada_units": _tiles(a["w_ada"][0]),
        "x_prompt": a["x_prompt"][0].reshape(NP, KT, P).transpose(2, 1, 0),
        "x_sample": a["x_sample"].reshape(NB * TB, KT, P).transpose(2, 1, 0),
        "c": np.concatenate([a["c_prompt"], a["c_sample"]]).reshape(NV, KT, P).transpose(2, 1, 0),
        "b_ada": a["b_ada"][0].reshape(NMOD * KT, P).T,
        "b_in": b_in.transpose(2, 0, 1),
        "vecs": vecs.reshape(8, KT, P).transpose(2, 0, 1),
        "w_dw": a["w_dw"][0].reshape(CW, KT, P).transpose(2, 1, 0),
        "w_if": w_in[:, 8 * D:].reshape(KT, P, 2 * H).transpose(1, 0, 2),
        "b_i": a["b_in"][0, 8 * D:8 * D + H].reshape(H, 1),
        "b_f": a["b_in"][0, 8 * D + H:].reshape(H, 1),
        "state_m": a["state_m"][0].T,
        "state_conv": a["state_conv"][0].reshape(NB, PAST, KT, P).transpose(2, 3, 0, 1),
        "state": state.transpose(0, 1, 3, 2, 4),
    }
    outs = {"y": (KT, P, NT), "conv_p": (KT, P, PAST), "conv_s": (KT, P, NB, PAST), "m": (H, 1 + NB),
            "C_p": (H, P, 2, C1), "C_s": (H, NB, P, 2, C1)}
    nc = bacc.Bacc("TRN2", target_bir_lowering=False, num_devices=1, dynamic_dma_scratch_size=64)
    arrays = {n: np.ascontiguousarray(v) for n, v in feats.items()}
    t_in = {n: nc.dram_tensor(n + "_dram", v.shape, F32, kind="ExternalInput").ap() for n, v in arrays.items()}
    t_out = {n: nc.dram_tensor(n + "_out", s, F32, kind="ExternalOutput").ap() for n, s in outs.items()}
    trunk(nc, t_in, t_out)
    res = run_bass_kernel_spmd(nc, [{n + "_dram": v for n, v in arrays.items()}], core_ids=[0]).results[0]
    r = {n: np.asarray(res[n + "_out"]) for n in outs}
    y = r["y"].reshape(D, NT).T
    c_p = r["C_p"].transpose(0, 2, 1, 3).reshape(1, 1, H, HD, C1)
    c_s = r["C_s"].transpose(1, 0, 3, 2, 4).reshape(1, NB, H, HD, C1)
    c = np.ascontiguousarray
    return (c(y[:NP]).reshape(1, NP, D), c(y[NP:]).reshape(NB, TB, D),
            c(r["conv_p"].reshape(D, PAST).T).reshape(1, 1, PAST, D),
            c(c_p[..., :HD].swapaxes(-1, -2)), c(c_p[..., HD]), c(r["m"][:, 0]).reshape(1, 1, H),
            c(r["conv_s"].reshape(D, NB, PAST).transpose(1, 2, 0)).reshape(1, NB, PAST, D),
            c(c_s[..., :HD].swapaxes(-1, -2)), c(c_s[..., HD]), c(r["m"][:, 1:].T).reshape(1, NB, H))
```
